# Optimizing a Trainium2 kernel written in Bass

```python
import math
import jax, jax.numpy as jnp
from jax import lax
import numpy as np

D_MODEL = 1024
BATCH = 1
SEQ = 512
DEPTH = 1

N_MOD = 6
GLA_HEADS = 4
GLA_DK = D_MODEL // 16
GLA_DV = D_MODEL // 8
GLA_WIDTH = GLA_HEADS * GLA_DV
GLA_LOWRANK = 16
GLA_GATE_NORM = 16.0
GLA_CHUNK = 64
FOX_HEADS = 8
FOX_DH = D_MODEL // 16
FOX_WIDTH = FOX_HEADS * FOX_DH
FOX_QBLOCK = 128
MIX_WIDTH = GLA_WIDTH + FOX_WIDTH
SPLIT_SIZES = (GLA_HEADS * GLA_DK, GLA_HEADS * GLA_DK, GLA_WIDTH, GLA_WIDTH, GLA_LOWRANK,
               FOX_WIDTH, FOX_WIDTH, FOX_WIDTH, FOX_HEADS)
IN_COLS = sum(SPLIT_SIZES)
N_EXPERTS = 32
TOP_K = 4
D_FF = D_MODEL
SWIGLU_ALPHA = 1.702
SWIGLU_LIMIT = 7.0
MOE_BLOCK = 128
EPS = 1e-6

kernel_name = "hymba_gla_fox_moe_sandwich_adaln"

def rmsnorm(x, g):
    xf = x.astype(jnp.float32)
    y = xf * lax.rsqrt(jnp.mean(xf * xf, axis=-1, keepdims=True) + EPS)
    return (y * g.astype(jnp.float32)).astype(x.dtype)

def gla_chunked(q, k, v, log_a):
    B, S, H, K = q.shape
    V = v.shape[-1]
    N = S // GLA_CHUNK
    qc = q.reshape(B, N, GLA_CHUNK, H, K).astype(jnp.float32)
    kc = k.reshape(B, N, GLA_CHUNK, H, K).astype(jnp.float32)
    vc = v.reshape(B, N, GLA_CHUNK, H, V)
    b = jnp.cumsum(log_a.reshape(B, N, GLA_CHUNK, H, K), axis=2)
    b_last = b[:, :, -1:]
    q_t = qc * jnp.exp(b) * (K ** -0.5)
    k_t = kc * jnp.exp(-b)
    k_d = kc * jnp.exp(b_last - b)
    causal = jnp.tril(jnp.ones((GLA_CHUNK, GLA_CHUNK), dtype=bool))
    att = jnp.einsum('bnihk,bnjhk->bnhij', q_t, k_t)
    att = jnp.where(causal, att, 0.0)
    o_intra = jnp.einsum('bnhij,bnjhv->bnihv', att, vc)
    kv = jnp.einsum('bnjhk,bnjhv->bnhkv', k_d, vc)
    decay = jnp.exp(b_last[:, :, 0])

    def step(state, inp):
        dec, kv_n = inp
        return dec[..., None] * state + kv_n, state

    init = jnp.zeros((B, H, K, V), jnp.float32)
    _, s_prev = lax.scan(step, init, (jnp.moveaxis(decay, 1, 0), jnp.moveaxis(kv, 1, 0)))
    s_prev = jnp.moveaxis(s_prev, 0, 1)
    o_inter = jnp.einsum('bnihk,bnhkv->bnihv', q_t, s_prev)
    return (o_intra + o_inter).reshape(B, S, H, V)

def forgetting_attention(q, k, v, log_f):
    B, S, H, D = q.shape
    Ft = jnp.moveaxis(jnp.cumsum(log_f.astype(jnp.float32), axis=1), 1, 2)
    scale = D ** -0.5
    outs = []
    for i in range(S // FOX_QBLOCK):
        lo, hi = i * FOX_QBLOCK, (i + 1) * FOX_QBLOCK
        s = jnp.einsum('bqhd,bkhd->bhqk', q[:, lo:hi], k[:, :hi]).astype(jnp.float32) * scale
        s = s + (Ft[:, :, lo:hi, None] - Ft[:, :, None, :hi])
        mask = jnp.arange(hi)[None, :] <= (lo + jnp.arange(FOX_QBLOCK))[:, None]
        s = jnp.where(mask, s, -jnp.inf)
        p = jax.nn.softmax(s, axis=-1)
        outs.append(jnp.einsum('bhqk,bkhd->bqhd', p.astype(v.dtype), v[:, :hi]))
    return jnp.concatenate(outs, axis=1)

def token_mixer(h, w_in, w_gk2, b_gk, gla_norm_gain, b_f, w_o):
    B, S, _ = h.shape
    proj = h @ w_in
    idx = list(np.cumsum(SPLIT_SIZES)[:-1])
    qg, kg, vg, gg, zg, qf, kf, vf, ff = jnp.split(proj, idx, axis=-1)
    gk = zg @ w_gk2 + b_gk
    log_a = jax.nn.log_sigmoid(gk.astype(jnp.float32)) / GLA_GATE_NORM
    o_gla = gla_chunked(qg.reshape(B, S, GLA_HEADS, GLA_DK),
                        kg.reshape(B, S, GLA_HEADS, GLA_DK),
                        vg.reshape(B, S, GLA_HEADS, GLA_DV),
                        log_a.reshape(B, S, GLA_HEADS, GLA_DK))
    o_gla = rmsnorm(o_gla, gla_norm_gain.reshape(GLA_HEADS, GLA_DV)).reshape(B, S, GLA_WIDTH)
    o_gla = (o_gla * jax.nn.silu(gg)).astype(h.dtype)
    log_f = jax.nn.log_sigmoid((ff + b_f).astype(jnp.float32))
    o_fox = forgetting_attention(qf.reshape(B, S, FOX_HEADS, FOX_DH),
                                 kf.reshape(B, S, FOX_HEADS, FOX_DH),
                                 vf.reshape(B, S, FOX_HEADS, FOX_DH), log_f)
    o_fox = o_fox.reshape(B, S, FOX_WIDTH).astype(h.dtype)
    return jnp.concatenate([o_gla, o_fox], axis=-1) @ w_o

def moe(h2d, w_router, b_router, w_e_in, b_e_in, w_e_out, b_e_out):
    T, D = h2d.shape
    logits = (h2d @ w_router + b_router).astype(jnp.float32)
    top_vals, top_idx = lax.top_k(logits, TOP_K)
    gates = jax.nn.softmax(top_vals, axis=-1)
    TK = T * TOP_K
    e_flat = top_idx.reshape(TK).astype(jnp.int32)
    g_flat = gates.reshape(TK)
    tok_flat = jnp.arange(TK, dtype=jnp.int32) // TOP_K
    order = jnp.argsort(e_flat)
    e_sorted, tok_sorted, g_sorted = e_flat[order], tok_flat[order], g_flat[order]
    counts = jnp.bincount(e_flat, length=N_EXPERTS)
    padded = ((counts + MOE_BLOCK - 1) // MOE_BLOCK) * MOE_BLOCK
    start = jnp.cumsum(counts) - counts
    pend = jnp.cumsum(padded)
    pstart = pend - padded
    dest = pstart[e_sorted] + (jnp.arange(TK, dtype=jnp.int32) - start[e_sorted])
    n_blocks = -(-TK // MOE_BLOCK) + N_EXPERTS
    P = n_blocks * MOE_BLOCK
    slot_tok = jnp.full((P,), T, jnp.int32).at[dest].set(tok_sorted)
    block_expert = jnp.minimum(
        jnp.searchsorted(pend, jnp.arange(n_blocks) * MOE_BLOCK, side='right'), N_EXPERTS - 1)
    h_pad = jnp.concatenate([h2d, jnp.zeros((1, D), h2d.dtype)], axis=0)
    xb = h_pad[slot_tok].reshape(n_blocks, MOE_BLOCK, D)

    def expert_block(args):
        xblk, e = args
        u = xblk @ w_e_in[e] + b_e_in[e]
        glu, lin = u[:, :D_FF], u[:, D_FF:]
        glu = jnp.minimum(glu, SWIGLU_LIMIT)
        lin = jnp.clip(lin, -SWIGLU_LIMIT, SWIGLU_LIMIT)
        a = glu * jax.nn.sigmoid(SWIGLU_ALPHA * glu) * (lin + 1.0)
        return a @ w_e_out[e] + b_e_out[e]

    yb = lax.map(expert_block, (xb, block_expert)).reshape(P, D)
    y_slot = yb[dest] * g_sorted[:, None].astype(yb.dtype)
    return jax.ops.segment_sum(y_slot, tok_sorted, num_segments=T)

def setup_inputs(seed: int = 0) -> dict:
    key = jax.random.key(seed)
    ks = jax.random.split(key, 24)
    f32 = jnp.float32
    n = lambda k, shape, s: jax.random.normal(k, shape, f32) * s
    D = D_MODEL
    return {
        "x": n(ks[0], (BATCH, SEQ, D), 1.0),
        "c": n(ks[1], (BATCH, D), 1.0),
        "w_ada": n(ks[2], (D, N_MOD * D), 0.5 * D ** -0.5),
        "b_ada": n(ks[3], (N_MOD * D,), 0.1),
        "attn_pre_gain": 1.0 + n(ks[4], (D,), 0.02),
        "attn_post_gain": 1.0 + n(ks[5], (D,), 0.02),
        "w_in": n(ks[6], (D, IN_COLS), D ** -0.5),
        "w_gk2": n(ks[7], (GLA_LOWRANK, GLA_HEADS * GLA_DK), GLA_LOWRANK ** -0.5),
        "b_gk": n(ks[8], (GLA_HEADS * GLA_DK,), 0.1),
        "gla_norm_gain": 1.0 + n(ks[9], (GLA_WIDTH,), 0.02),
        "b_f": 3.0 + n(ks[10], (FOX_HEADS,), 0.5),
        "w_o": n(ks[11], (MIX_WIDTH, D), MIX_WIDTH ** -0.5),
        "mlp_pre_gain": 1.0 + n(ks[12], (D,), 0.02),
        "mlp_post_gain": 1.0 + n(ks[13], (D,), 0.02),
        "w_router": n(ks[14], (D, N_EXPERTS), D ** -0.5),
        "b_router": n(ks[15], (N_EXPERTS,), 0.01),
        "w_e_in": n(ks[16], (N_EXPERTS, D, 2 * D_FF), D ** -0.5),
        "b_e_in": n(ks[17], (N_EXPERTS, 2 * D_FF), 0.01),
        "w_e_out": n(ks[18], (N_EXPERTS, D_FF, D), D_FF ** -0.5),
        "b_e_out": n(ks[19], (N_EXPERTS, D), 0.01),
    }

def reference(x, c, w_ada, b_ada, attn_pre_gain, attn_post_gain, w_in, w_gk2, b_gk,
              gla_norm_gain, b_f, w_o, mlp_pre_gain, mlp_post_gain, w_router, b_router,
              w_e_in, b_e_in, w_e_out, b_e_out):
    B, S, D = x.shape
    mod = jax.nn.silu(c) @ w_ada + b_ada
    shift_a, scale_a, gate_a, shift_m, scale_m, gate_m = [m[:, None, :] for m in jnp.split(mod, N_MOD, axis=-1)]
    for _ in range(DEPTH):
        h = rmsnorm(x, attn_pre_gain) * (1.0 + scale_a) + shift_a
        y = token_mixer(h, w_in, w_gk2, b_gk, gla_norm_gain, b_f, w_o)
        x = x + gate_a * rmsnorm(y, attn_post_gain)
        h = rmsnorm(x, mlp_pre_gain) * (1.0 + scale_m) + shift_m
        y = moe(h.reshape(B * S, D), w_router, b_router, w_e_in, b_e_in, w_e_out, b_e_out).reshape(B, S, D)
        x = x + gate_m * rmsnorm(y, mlp_post_gain)
    return x


_drawn_inputs = setup_inputs


def setup_inputs(seed=0):
    import zlib

    import numpy as np

    out = dict(_drawn_inputs(seed))
    spreads = {}
    factors = {'attn_post_gain': 3.683,
     'b_gk': 2.773,
     'gla_norm_gain': 4.514,
     'mlp_post_gain': 8.0,
     'b_router': 3.221,
     'b_e_in': 8.0,
     'b_e_out': 8.0}
    for name, (base, spread) in spreads.items():
        noise = np.random.default_rng([zlib.crc32(name.encode()), seed]).standard_normal(out[name].shape)
        drawn = base * np.exp(spread * noise) if base else spread * noise
        out[name] = __import__('jax').numpy.asarray(drawn.astype(out[name].dtype))
    for name, factor in factors.items():
        out[name] = (out[name] * factor).astype(out[name].dtype)
    return out
```

```python
from contextlib import ExitStack

import concourse.bass as bass
from concourse import mybir

F32 = mybir.dt.float32
BF16 = mybir.dt.bfloat16
I32 = mybir.dt.int32
ALU = mybir.AluOpType
ACT = mybir.ActivationFunctionType
AX = mybir.AxisListType

P = 128
D = 1024
KT = D // P
T = 512
TT = T // P
EPS = 1e-6
GH, GK, GV, CH = 4, 64, 128, 64
FH, FD = 8, 64
GLA_NORM = 16.0
LR = 16
C_QG, C_KG, C_VG, C_GG, C_Z, C_QF, C_KF, C_VF, C_FF = 0, 256, 512, 1024, 1536, 1552, 2064, 2576, 3088
E = 32
TOPK = 4
ALPHA, LIMIT = 1.702, 7.0
BLK = 64
OVER = T * TOPK // P - 1
NV = E + OVER
NCOL = NV + 1
SLOT = 2048
NEG = -1.0e30


def build(nc, x, c, w_ada, b_ada, attn_pre_gain, attn_post_gain, w_in, w_gk2, b_gk, gla_norm_gain,
          b_f, w_o, mlp_pre_gain, mlp_post_gain, w_router, b_router, w_e_in, b_e_in, w_e_out,
          b_e_out, out):
    h_dram = nc.dram_tensor("h_rows", (T, D), F32).ap()
    y_dram = nc.dram_tensor("expert_rows", (T * TOPK + P, D), F32).ap()
    vec_dram = nc.dram_tensor("norm_vectors", (4, D), F32).ap()
    bias_dram = nc.dram_tensor("bias_parts", (E, 3, 3 * D), BF16).ap()

    with ExitStack() as ctx:
        def sb(name, shape, dt=F32):
            return ctx.enter_context(nc.sbuf_tensor(name, shape, dt))

        def sem(name):
            return ctx.enter_context(nc.semaphore(name))

        ring = sb("ring", [P, 12 * SLOT])
        region_x = sb("region_x", [P, TT * D])
        region_h = sb("region_h", [P, TT * D])
        region_1 = sb("region_1", [P, TT * D])
        region_m = sb("region_m", [P, 8192])
        bank = ctx.enter_context(nc.psum_tensor("bank", [P, 8, 512], F32))

        def chunk_buf(s):
            return ring[:, (s % 3) * 2 * SLOT:(s % 3 + 1) * 2 * SLOT].rearrange("p (k n) -> p k n", k=KT)

        def slot(j):
            return ring[:, j * SLOT:(j + 1) * SLOT]

        qa = ring[0:66, 6 * SLOT:8 * SLOT].rearrange("p (h t) -> p h t", h=FH)
        ka = ring[0:66, 8 * SLOT:10 * SLOT].rearrange("p (h t) -> p h t", h=FH)
        vf = slot(10).rearrange("p (i n) -> p i n", i=TT)
        vg = slot(11).rearrange("p (i n) -> p i n", i=TT)
        wo_sb = ring[:, 0:4 * SLOT].rearrange("p (k n) -> p k n", k=KT)

        x_sb = region_x[:, :].rearrange("p (i n) -> p i n", i=TT)
        qg_raw = region_x[:, 0:1024].rearrange("p (a t) -> p a t", a=2)
        kg_raw = region_x[:, 1024:2048].rearrange("p (a t) -> p a t", a=2)
        cumT = region_x[:, 2048:3072].rearrange("p (a t) -> p a t", a=2)
        gtmp = region_x[:, 3072:4096].rearrange("p (a t) -> p a t", a=2)
        mix = x_sb
        h2 = region_x[:, 0:2048].rearrange("p (b n) -> p b n", b=2)
        h2T = region_x[:, 2048:4096].rearrange("p (b k t) -> p b k t", b=2, k=KT)
        bias3 = ring[0:E, 6 * SLOT:6 * SLOT + 9 * D // 2].bitcast(BF16).rearrange("p (j n) -> p j n", j=3)
        hT = region_h[:, :].rearrange("p (k t) -> p k t", k=KT)
        mixT = hT
        bias_raw = region_1[0:E, 0:3 * D]
        prob = region_1[:, 0:1024].rearrange("p (b n) -> p b n", b=2)
        probT = region_1[:, 1024:2048].rearrange("p (b n) -> p b n", b=2)
        attz = region_1[:, 2048:3072].rearrange("p (b h n) -> p b h n", b=2, h=GH)
        osb = region_1[:, 3072:3584]
        osq = region_1[:, 3584:4096]
        zf = region_1[0:40, 3072:3584]
        x1 = region_1[:, :].rearrange("p (i n) -> p i n", i=TT)
        gs = region_m[:, 0:2048].rearrange("p (i n) -> p i n", i=TT)
        qtp = region_m[:, 2048:4096].rearrange("p (h t) -> p h t", h=GH)
        ktT = region_m[:, 4096:5120].rearrange("p (a t) -> p a t", a=2)
        kdT = region_m[:, 5120:6144].rearrange("p (a t) -> p a t", a=2)
        etmp = region_m[:, 6144:7168].rearrange("p (a t) -> p a t", a=2)
        kdz = region_m[:, 7168:8192].rearrange("p (b c n) -> p b c n", b=2, c=2)
        ytmp = region_m[:, 2048:3072]
        ynorm = region_m[:, 3072:4096]
        xg = region_m[:, 0:1024]
        xT = region_m[:, 1024:2048].rearrange("p (k s) -> p k s", k=KT)
        act_a = region_m[:, 2048:3072].rearrange("p (b n) -> p b n", b=2)
        aT = region_m[:, 3072:4096].rearrange("p (b c s) -> p b c s", b=2, c=4)
        y_sb = region_m[:, 4096:5120].rearrange("p (b n) -> p b n", b=2)
        g_sb = region_m[:, 5120:6144].rearrange("p (b n) -> p b n", b=2)
        s_sb = region_m[:, 6144:7168].rearrange("p (b n) -> p b n", b=2)
        l_sb = region_m[:, 7168:8192].rearrange("p (b n) -> p b n", b=2)

        state = sb("state", [P, 4, GH, GV])
        pga = sb("pga", [P, D])
        gm = sb("gm", [P, D])
        sm = sb("sm", [P, D])
        ident = sb("ident", [P, P])
        ones = sb("ones", [P, P])
        before = sb("before", [P, P])
        iota = sb("iota", [P, P])
        identb = sb("identb", [P, P], BF16)
        maskb = sb("maskb", [P, P], BF16)
        ones3 = sb("ones3", [3, BLK], BF16)
        tid = sb("tid", [P, TT])
        scan_reset = sb("scan_reset", [P, T], BF16)
        route_reset = sb("route_reset", [P, P], BF16)
        half_pow = sb("half_pow", [P, 4])
        cs_pad = sb("cs_pad", [P, KT, 32])
        crow = region_m[0:KT, 448:576]
        vrows = region_m[0:82, 320:448]
        vcol = sb("vcol", [P, 82])
        modT = sb("modT", [P, 48])
        ga = sb("ga", [P, KT])
        cols = sb("cols", [P, 4, KT])
        mrow = sb("mrow", [P, 2, P])
        gain_bc = sb("gain_bc", [P, T])
        br_bc = sb("br_bc", [P, E])
        wzf = region_m[:, 0:320].rearrange("p (k n) -> p k n", k=KT)
        wgk = region_1[0:LR, 3584:3840]
        bf_col = sb("bf_col", [40, 1])
        fwork = state[0:40, :, :, :].rearrange("p a h v -> p a (h v)")
        w_r = sb("w_r", [P, KT, E])
        stat = sb("stat", [P, 64])
        rsum = sb("rsum", [P, 32])
        nmax = sb("nmax", [P, 4])
        dec = sb("dec", [P, 2, T // CH])
        lg = sb("lg", [P, TT, E])
        gate_k = sb("gate_k", [P, 16])
        slot_k = sb("slot_k", [P, 16], I32)
        tok = sb("tok", [P, NCOL], I32)
        tok_now = sb("tok_now", [P, 1], I32)
        flags = sb("flags", [1, 64], I32)
        row_start = sb("row_start", [1, 48], I32)
        over_e = sb("over_e", [1, 16], I32)
        over_n = sb("over_n", [1, 1], I32)
        bup = state[0:3, 0:2, :, :].rearrange("p a h v -> p (a h v)").bitcast(BF16)
        bdn = state[0:3, 2:3, :, :].rearrange("p a h v -> p (a h v)").bitcast(BF16)
        rcp = sb("rcp", [P, FH])
        mark = sb("mark", [P, 2])

        WORK = "sub ex eq eqc gt mask rk pos over lo vis gate".split()

        def rw(name):
            j = WORK.index(name)
            return region_h[:, j * P:(j + 1) * P].rearrange("p (i e) -> p i e", i=TT)

        sel4 = region_h[:, 1536:2048].rearrange("p (i k e) -> p i k e", i=TT, k=TOPK)
        prod4 = region_h[:, 2048:2560].rearrange("p (i k e) -> p i k e", i=TT, k=TOPK)
        hot_v = region_h[:, 2560:3328].rearrange("p (q n) -> p q n", q=16)
        small = region_h[:, 3328:4096]
        hot_l = region_x[:, 2048:4096].rearrange("p (q n) -> p q n", q=16)

        def row_buf(q):
            at = q * SLOT if q < 12 else (q - 12) * SLOT + D
            return ring[:, at:at + D]

        def fin_y(i):
            return row_buf(4 * i)

        names = """consts small_in crow_in x_in stream0 stream1 stream2 vr_done
            vcol_ready cs_ready csT_done csT_ev ada_mm ada_row ada_tr ada_col x_sq x_ms x_rstd x_norm xt_mm
            ga_ready ht_act ht_dve proj_mm ev_act ev_dve sig_done dve_step act_step pool_step
            fx_ln fx_cum fx_in gk_abs gk_ln cum_done enb_done dd_done dk_done
            dec_done gla_ready gs_ready bias_in bias_split bias_out cols_ready colT_mm vec_ready vec_out bc_in 
            kd_mm kd_ev att_mm att_cp att_ready kv_mm st_done go_mm go_ev go_ms go_rstd mixg
            s_done max_done exp_done pt_done pt_ev pv_done mixf mt_mm mt_ev wo_in x1_in wo_mm wo_sq wo_ms wo_rstd
            x1_done x1_sq x1_ms x1_rstd h2_done h2_store0 h2_store1 h2t_mm h2t_ev lg_mm lg_done r_sub r_exp r_mask pos_mm
            hot_ready tab_mm flags_ready tok_ready
            up_bias_in dn_bias_in up_bias_used dn_bias_used win_used wout_used gathered tok_copied xtr_done
            xt_ready u_free g_ready s_ready a_ready atr_done at_ready y_evac y_stored
            fin_sq fin_ms fin_rstd fin_done out_done yacc lin_done""".split()
        S = {n: sem(n) for n in names}
        fin_in = [sem(f"fin_in{q}") for q in range(16)]
        w_slot = [sem(f"w_slot{j}") for j in range(12)]
        h2_store = [S["h2_store0"], S["h2_store1"]]
        stream = [S["stream0"], S["stream1"], S["stream2"]]

        PROJ = [C_QG, C_GG, C_VG, C_KF, C_QF, C_VF]
        chunks = [("ada", n) for n in range(4)]
        for m, at in enumerate(PROJ):
            chunks += [("in", at), ("ada", 4 + m)]
        chunks += [("ada", 10), ("ada", 11)]
        at_chunk = {ch: s for s, ch in enumerate(chunks)}

        outs = [("zf", 0, "act")]
        outs += [("qg", a, "act") for a in range(2)] + [("kg", a, "act") for a in range(2)]
        outs += [("gk", a, "dve") for a in range(2)]
        outs += [("gg", i, "dve") for i in range(TT)] + [("vg", i, "act") for i in range(TT)]
        outs += [("kf", a, "act" if a % 2 else "dve") for a in range(4)]
        outs += [("qf", a, "act" if a % 2 else "dve") for a in range(4)]
        outs += [("vf", i, "act" if i % 2 else "dve") for i in range(TT)]
        out_at = {(k, a): j for j, (k, a, _) in enumerate(outs)}

        lasts = [("kg", 1), ("gg", 3), ("vg", 3), ("kf", 3), ("qf", 3), ("vf", 3)]
        ada_behind = {4 + m: out_at[last] for m, last in enumerate(lasts)}
        ada_turned = {n: min(j + 2, len(outs) - 1) for n, j in ada_behind.items()}

        def ada_bank(n):
            return n % 2 + (4 if n >= 4 else 0)

        def taken(j):
            who = outs[j][2]
            return S["ev_" + who], sum(1 for o in outs[:j + 1] if o[2] == who)

        def wait_out(eng, kind):
            for who in ("act", "dve"):
                js = [j for j, o in enumerate(outs) if o[0] == kind and o[2] == who]
                if js:
                    eng.wait_ge(*taken(js[-1]))

        def wait_used(eng, s):
            kind, n = chunks[s]
            if kind == "ada":
                eng.wait_ge(S["ada_mm"], n + 1)
            else:
                eng.wait_ge(S["proj_mm"], out_at[lasts[PROJ.index(n)]] + 1)

        units = [(qi, h) for qi in range(TT) for h in range(FH)]
        block = ctx.enter_context(nc.Block())

        @block.sync
        def _(sp):
            sp.dma_start(crow[:, :], c.rearrange("b (k p) -> (b k) p", p=P)).then_inc(S["crow_in"], 16)
            vectors = [
                (vrows[0:48, :], b_ada.rearrange("(k p) -> k p", p=P)),
                (vrows[48:56, :], attn_pre_gain.rearrange("(k p) -> k p", p=P)),
                (vrows[56:64, :], attn_post_gain.rearrange("(k p) -> k p", p=P)),
                (vrows[64:72, :], mlp_pre_gain.rearrange("(k p) -> k p", p=P)),
                (vrows[72:80, :], mlp_post_gain.rearrange("(k p) -> k p", p=P)),
                (vrows[80:82, :], b_gk.rearrange("(k p) -> k p", p=P)),
            ]
            for dst, src in vectors:
                sp.dma_start(dst, src).then_inc(S["small_in"], 16)
            sp.dma_start(bias_raw[:, 0:2 * D], b_e_in).then_inc(S["bias_in"], 16)
            sp.dma_start(bias_raw[:, 2 * D:3 * D], b_e_out).then_inc(S["bias_in"], 16)

            def load_chunk(s):
                kind, n = chunks[s]
                if s >= 3:
                    wait_used(sp, s - 3)
                src = w_ada[:, n * 512:(n + 1) * 512] if kind == "ada" else w_in[:, n:n + 512]
                sp.dma_start(chunk_buf(s), src.rearrange("(k p) n -> p k n", p=P)).then_inc(stream[s % 3], 16)

            load_chunk(0)
            sp.dma_start(x_sb, x.rearrange("b (i p) n -> p (b i) n", p=P)).then_inc(S["x_in"], 16)
            load_chunk(1)
            load_chunk(2)
            load_chunk(3)
            w_in_k = w_in.rearrange("(k p) n -> p k n", p=P)
            sp.wait_ge(S["consts"], 1)
            sp.dma_start(wzf[:, :, 0:LR], w_in_k[:, :, C_Z:C_Z + LR]).then_inc(S["fx_in"], 16)
            sp.dma_start(wzf[:, :, 32:40], w_in_k[:, :, C_FF:C_FF + FH]).then_inc(S["fx_in"], 16)
            sp.dma_start(bf_col[32:40, :], b_f.rearrange("(h a) -> h a", a=1)).then_inc(S["fx_in"], 16)
            sp.dma_start(wgk[:, :], w_gk2).then_inc(S["fx_in"], 16)
            sp.dma_start(gain_bc[:, :], gla_norm_gain.rearrange("(a n) -> a n", a=1).to_broadcast([P, T])).then_inc(S["fx_in"], 16)
            sp.dma_start(br_bc[:, :], b_router.rearrange("(a n) -> a n", a=1).to_broadcast([P, E])).then_inc(S["fx_in"], 16)
            sp.dma_start(w_r[:, :, :], w_router.rearrange("(k p) n -> p k n", p=P)).then_inc(S["fx_in"], 16)
            for s in range(4, len(chunks)):
                load_chunk(s)
                if s == 6:
                    sp.wait_ge(S["bias_split"], 1)
                    sp.dma_start(bias_dram, bias3).then_inc(S["bias_out"], 16)
                    sp.wait_ge(S["fx_cum"], 2)
                    sp.wait_ge(S["consts"], 2)
                    sp.dma_start(qa[65:66, :, :], fwork[32:40, 2, :]).then_inc(S["fx_in"], 16)
                    sp.dma_start(ka[64:65, :, :], fwork[32:40, 3, :]).then_inc(S["fx_in"], 16)
            wait_used(sp, len(chunks) - 2)
            sp.dma_start(wo_sb, w_o.rearrange("(k p) n -> p k n", p=P)).then_inc(S["wo_in"], 16)

            def load_up(e, j):
                sp.dma_start(slot(j), w_e_in[e, j * P:(j + 1) * P, :]).then_inc(w_slot[j], 16)

            def load_down(e, j):
                src = w_e_out[e, j * 2 * P:(j + 1) * 2 * P, :].rearrange("(k p) n -> p k n", p=P)
                sp.dma_start(slot(8 + j).rearrange("p (k n) -> p k n", k=2), src).then_inc(w_slot[8 + j], 16)

            sp.wait_ge(S["vec_ready"], 1)
            sp.dma_start(vec_dram.rearrange("a (k p) -> (a k) p", p=P), mrow[0:32, 0, :]).then_inc(S["vec_out"], 16)
            sp.wait_ge(S["vec_out"], 16)
            for n, dst in enumerate((pga, gm, sm)):
                sp.dma_start(dst[:, :], vec_dram[n:n + 1, :].to_broadcast([P, D])).then_inc(S["bc_in"], 16)

            wait_used(sp, len(chunks) - 1)
            load_up(0, 4)
            load_up(0, 5)
            sp.wait_ge(S["pv_done"], len(units))
            sp.wait_ge(S["bias_out"], 16)
            sp.dma_start(bup, bias_dram[0, :, 0:2 * D]).then_inc(S["up_bias_in"], 16)
            sp.dma_start(bdn, bias_dram[0, :, 2 * D:3 * D]).then_inc(S["dn_bias_in"], 16)
            sp.dma_start(x1, x.rearrange("b (i p) n -> p (b i) n", p=P)).then_inc(S["x1_in"], 16)
            for j in (6, 7):
                load_up(0, j)
            for j in range(4):
                load_down(0, j)
            sp.wait_ge(S["wo_mm"], TT)
            for j in range(4):
                load_up(0, j)

            sp.wait_ge(S["h2_done"], TT)
            sp.dma_start(gm[:, :], vec_dram[3:4, :].to_broadcast([P, D])).then_inc(S["bc_in"], 16)

            def up_weights(e, v):
                sp.wait_ge(S["up_bias_used"], v)
                sp.dma_start(bup, bias_dram[e, :, 0:2 * D]).then_inc(S["up_bias_in"], 16)
                for j in range(8):
                    sp.wait_ge(S["win_used"], (v - 1) * 8 + j + 1)
                    load_up(e, j)

            def down_weights(e, v):
                sp.wait_ge(S["dn_bias_used"], v)
                sp.dma_start(bdn, bias_dram[e, :, 2 * D:3 * D]).then_inc(S["dn_bias_in"], 16)
                for j in range(4):
                    sp.wait_ge(S["wout_used"], (v - 1) * 4 + j + 1)
                    load_down(e, j)

            up_weights(1, 1)
            with sp.Fori(2, E) as v:
                up_weights(v, v)
                down_weights(v - 1, v - 1)
            down_weights(E - 1, E - 1)
            sp.wait_ge(S["flags_ready"], 2)
            with sp.Fori(0, OVER) as j:
                n = sp.value_load(flags[0:1, bass.ds(j + E, 1)], min_val=0, max_val=2)
                with sp.If(n > 0):
                    e = sp.value_load(over_e[0:1, bass.ds(j, 1)], min_val=0, max_val=E - 1)
                    up_weights(e, j + E)
                    down_weights(e, j + E)

        @block.gpsimd
        def _(pool):
            g = nc.gpsimd
            step = [0]

            def link(ins):
                step[0] += 1
                ins.then_inc(S["pool_step"], 1)
                pool.wait_ge(S["pool_step"], step[0])

            link(g.memset(wzf[:, :, :], 0.0))
            link(g.memset(cs_pad[:, :, :], 0.0))
            link(g.memset(ident[:, :], 0.0))
            link(g.affine_select(out=ident[:, :], in_=ident[:, :], compare_op=ALU.not_equal, fill=1.0, base=0,
                                 pattern=[[-1, P]], channel_multiplier=1))
            link(g.memset(half_pow[:, :], -0.5))
            link(g.iota(tid[:, :], pattern=[[P, TT]], base=0, channel_multiplier=1, allow_small_or_imprecise_dtypes=True))
            g.memset(ones[:, :], 1.0).then_inc(S["consts"], 1)

            def power(dst, src, n):
                return g.tensor_tensor(out=dst, in0=src, in1=half_pow[:, 0:n], op=ALU.pow)

            for i in range(TT):
                pool.wait_ge(S["x_ms"], i + 1)
                power(stat[:, i:i + 1], stat[:, 4 + i:5 + i], 1).then_inc(S["x_rstd"], 1)
            link(g.memset(maskb[:, :], 0.0))
            link(g.affine_select(out=maskb[:, :], in_=maskb[:, :], compare_op=ALU.is_ge, fill=NEG, base=0,
                                 pattern=[[-1, P]], channel_multiplier=1))
            link(g.tensor_copy(identb[:, :], ident[:, :]))
            link(g.memset(before[:, :], 1.0))
            link(g.affine_select(out=before[:, :], in_=before[:, :], compare_op=ALU.is_ge, fill=0.0, base=-1,
                                 pattern=[[1, P]], channel_multiplier=-1))
            link(g.iota(iota[:, :], pattern=[[1, P]], base=0, channel_multiplier=0, allow_small_or_imprecise_dtypes=True))
            link(g.memset(scan_reset[:, :], 1.0))
            link(g.memset(scan_reset[:, :].rearrange("p (n c) -> p n c", c=CH)[:, :, 0:1], 0.0))
            link(g.memset(route_reset[:, :], 1.0))
            link(g.memset(route_reset[:, :].rearrange("p (n c) -> p n c", c=E)[:, :, 0:1], 0.0))
            link(g.memset(ones3[:, :], 1.0))
            pool.wait_ge(S["bias_out"], 16)
            link(g.memset(qa[64:66, :, :], 1.0))
            link(g.memset(ka[64:66, :, :], 1.0))
            link(g.memset(kdz[:, :, :, :], 0.0))
            link(g.memset(qtp[:, :, :], 0.0))
            g.memset(stat[:, 62:63], 0.0).then_inc(S["consts"], 1)
            pool.wait_ge(S["fx_in"], 16 * 7)
            for i in range(TT):
                pool.wait_ge(*taken(out_at[("gg", i)]))
                g.tensor_tensor(out=gs[:, i, :], in0=gs[:, i, :], in1=gain_bc[:, :], op=ALU.mult).then_inc(S["gs_ready"], 1)
            pool.wait_ge(S["bias_split"], 1)
            link(g.memset(attz[:, :, :, :], 0.0))
            pool.wait_ge(S["fx_in"], 16 * 9)
            link(g.memset(state[:, :, :, :], 0.0))
            g.memset(stat[:, 63:64], 0.0).then_inc(S["consts"], 1)
            for i in range(TT):
                pool.wait_ge(S["att_cp"], i + 1)
                g.affine_select(out=attz[:, i % 2, :, :], in_=attz[:, i % 2, :, :], compare_op=ALU.is_ge, fill=0.0,
                                base=0, pattern=[[0, GH], [1, P]], channel_multiplier=-1).then_inc(S["att_ready"], 1)
                if i >= 1:
                    pool.wait_ge(S["go_ms"], i)
                    power(stat[:, 8 + 4 * (i - 1):12 + 4 * (i - 1)], stat[:, 24 + 4 * (i - 1):28 + 4 * (i - 1)], 4).then_inc(S["go_rstd"], 1)
            pool.wait_ge(S["go_ms"], TT)
            power(stat[:, 20:24], stat[:, 36:40], 4).then_inc(S["go_rstd"], 1)
            for i in range(TT):
                pool.wait_ge(S["wo_ms"], i + 1)
                power(stat[:, 40 + i:41 + i], stat[:, 44 + i:45 + i], 1).then_inc(S["wo_rstd"], 1)
                pool.wait_ge(S["x1_ms"], i + 1)
                power(stat[:, 48 + i:49 + i], stat[:, 52 + i:53 + i], 1).then_inc(S["x1_rstd"], 1)

            def gather(v):
                g.tensor_copy(tok_now[:, :], tok[:, bass.ds(v, 1)]).then_inc(S["tok_copied"], 1)
                pool.wait_ge(S["tok_copied"], v + 1)
                g.tensor_tensor(mark[:, 0:1], half_pow[:, 0:1], half_pow[:, 1:2], ALU.mult)
                g.indirect_dma_start(out=xg[:, :], out_offset=None, in_=h_dram,
                                     in_offset=bass.IndirectOffsetOnAxis(ap=tok_now[:, 0:1], axis=0)).then_inc(S["gathered"], 16)

            pool.wait_ge(S["tok_ready"], 1)
            for b in range(2):
                pool.wait_ge(h2_store[b], 16 * TT // 2)
            gather(0)
            with pool.Fori(0, E) as v:
                pool.wait_ge(S["xtr_done"], 2 * v + 2)
                gather(v + 1)
            pool.wait_ge(S["flags_ready"], 2)
            with pool.Fori(0, OVER) as j:
                n = pool.value_load(flags[0:1, bass.ds(j + E, 1)], min_val=0, max_val=2)
                with pool.If(n > 0):
                    pool.wait_ge(S["xtr_done"], 2 * (j + E) + 2)
                    gather(j + E + 1)

            n = pool.value_load(over_n[0:1, 0:1], min_val=0, max_val=OVER)
            pool.wait_ge(S["y_stored"], 32 * (n + E))
            g.tensor_tensor(mark[:, 1:2], half_pow[:, 0:1], half_pow[:, 1:2], ALU.mult)
            for q in range(TT * TOPK):
                g.indirect_dma_start(out=row_buf(q), out_offset=None, in_=y_dram[0:T * TOPK, :],
                                     in_offset=bass.IndirectOffsetOnAxis(ap=slot_k[:, q:q + 1], axis=0)).then_inc(fin_in[q], 16)
            for i in range(TT):
                pool.wait_ge(S["fin_ms"], i + 1)
                power(stat[:, 56 + i:57 + i], stat[:, 4 + i:5 + i], 1).then_inc(S["fin_rstd"], 1)

        @block.scalar
        def _(act):
            a_ = nc.scalar
            step = [0]

            def link(ins):
                step[0] += 1
                ins.then_inc(S["act_step"], 1)
                act.wait_ge(S["act_step"], step[0])

            act.wait_ge(S["crow_in"], 16)
            a_.activation(fwork[0:KT, 0, 0:P], crow[:, :], ACT.Sigmoid).then_inc(S["cs_ready"], 1)
            act.wait_ge(S["x_in"], 16)
            for i in range(TT):
                a_.activation(region_h[:, i * D:(i + 1) * D], x_sb[:, i, :], ACT.Square, accum_out=stat[:, i:i + 1]).then_inc(S["x_sq"], 1)

            act.wait_ge(S["ga_ready"], 1)
            for k in range(1, KT, 2):
                act.wait_ge(S["xt_mm"], k + 1)
                a_.activation(hT[:, k, :], bank[:, 4 + k % 4, :], ACT.Identity, scale=ga[:, k:k + 1],
                              bias=modT[:, k:k + 1]).then_inc(S["ht_act"], 1)

            gg_done = 0
            for j, (kind, a, who) in enumerate(outs):
                src = bank[:, j % 4, :]
                if kind == "gk":
                    act.wait_ge(S["proj_mm"], j + 1)
                    a_.activation(etmp[:, a, :], src, ACT.Abs, bias=vcol[:, 80 + a:81 + a]).then_inc(S["gk_abs"], 1)
                    if a == 1:
                        act.wait_ge(S["gk_abs"], 2)
                        link(a_.activation(etmp[:, :, :], etmp[:, :, :], ACT.Exp, scale=-1.0))
                        a_.activation(etmp[:, :, :], etmp[:, :, :], ACT.Ln, bias=1.0).then_inc(S["gk_ln"], 1)
                        act.wait_ge(S["cum_done"], 2)
                        link(a_.activation(etmp[:, :, :], cumT[:, :, :], ACT.Exp, scale=1.0 / GLA_NORM))
                        a_.activation(dec[:, :, :], cumT.rearrange("p a (n c) -> p a n c", c=CH)[:, :, :, CH - 1],
                                      ACT.Exp, scale=1.0 / GLA_NORM).then_inc(S["dec_done"], 1)
                        act.wait_ge(S["dec_done"], 1)
                        a_.activation(gtmp[:, :, :], cumT[:, :, :], ACT.Exp, scale=-1.0 / GLA_NORM).then_inc(S["enb_done"], 1)
                        act.wait_ge(S["dd_done"], 2)
                        a_.activation(etmp[:, :, :], etmp[:, :, :], ACT.Exp, scale=1.0 / GLA_NORM).then_inc(S["dk_done"], 1)
                    continue
                if kind == "gg":
                    act.wait_ge(S["proj_mm"], j + 1)
                    if a >= 2:
                        act.wait_ge(*taken(out_at[("gg", a - 2)]))
                    a_.activation(prob[:, a % 2, :], src, ACT.Sigmoid).then_inc(S["sig_done"], 1)
                    continue
                if who != "act":
                    continue
                act.wait_ge(S["proj_mm"], j + 1)
                if kind == "zf":
                    a_.activation(zf[:, :], bank[0:40, j % 4, :], ACT.Copy).then_inc(S["ev_act"], 1)
                    act.wait_ge(S["ev_act"], 1)
                    act.wait_ge(S["fx_in"], 16 * 7)
                    act.wait_ge(S["csT_ev"], 1)
                    link(a_.activation(fwork[32:40, 0, :], zf[32:40, :], ACT.Abs, bias=bf_col[32:40, :]))
                    link(a_.activation(fwork[32:40, 0, :], fwork[32:40, 0, :], ACT.Exp, scale=-1.0))
                    a_.activation(fwork[32:40, 0, :], fwork[32:40, 0, :], ACT.Ln, bias=1.0).then_inc(S["fx_ln"], 1)
                elif kind in ("qg", "kg"):
                    if kind == "qg" and a == 0:
                        act.wait_ge(S["xt_mm"], KT)
                    dst = (qg_raw if kind == "qg" else kg_raw)[:, a, :]
                    a_.activation(dst, src, ACT.Copy).then_inc(S["ev_act"], 1)
                elif kind == "vg":
                    a_.activation(vg[:, a, :], src, ACT.Copy).then_inc(S["ev_act"], 1)
                elif kind == "vf":
                    a_.activation(vf[:, a, :], src, ACT.Copy).then_inc(S["ev_act"], 1)
                else:
                    dst, scale = (ka, 1.0) if kind == "kf" else (qa, FD ** -0.5)
                    act.wait_ge(S["consts"], 2)
                    a_.activation(dst[0:64, 2 * a, :], src[0:64, :], ACT.Copy, scale=scale)
                    a_.activation(dst[0:64, 2 * a + 1, :], src[64:128, :], ACT.Copy, scale=scale).then_inc(S["ev_act"], 1)

            def gla_scores(i):
                act.wait_ge(S["att_mm"], i + 1)
                act.wait_ge(S["consts"], 3)
                if i >= 2:
                    act.wait_ge(S["go_mm"], i - 1)
                src = bank[:, i % 2, :].rearrange("p (h n) -> p h n", h=GH)
                a_.activation(attz[0:64, i % 2, :, 0:64], src[0:64, :, 0:64], ACT.Copy)
                a_.activation(attz[64:128, i % 2, :, 64:128], src[64:128, :, 64:128], ACT.Copy).then_inc(S["att_cp"], 1)

            def gla_out(i):
                act.wait_ge(S["go_mm"], i + 1)
                if i >= 1:
                    act.wait_ge(S["mixg"], i)
                a_.activation(osb[:, :], bank[:, 5 + i % 2, :], ACT.Copy).then_inc(S["go_ev"], 1)

            gla_scores(0)
            for i in range(1, TT):
                gla_scores(i)
                gla_out(i - 1)

            def fox_exp(u):
                qi, h = units[u]
                act.wait_ge(S["max_done"], u + 1)
                if u >= 2:
                    act.wait_ge(S["pt_done"], u - 1)
                n = (qi + 1) * P
                a_.activation(prob[:, u % 2, 0:n], bank[:, u % 3, 0:n], ACT.Exp, bias=nmax[:, u % 4:u % 4 + 1],
                              accum_out=rsum[:, u:u + 1]).then_inc(S["exp_done"], 1)

            def fox_take(u):
                qi, h = units[u]
                act.wait_ge(S["pt_done"], u + 1)
                if u >= 2:
                    act.wait_ge(S["pv_done"], u - 1)
                n = (qi + 1) * P
                a_.activation(probT[:, u % 2, 0:n], bank[:, 3 + u % 2, 0:n], ACT.Copy).then_inc(S["pt_ev"], 1)

            fox_exp(0)
            gla_out(TT - 1)
            for u in range(1, len(units)):
                fox_exp(u)
                fox_take(u - 1)
            fox_take(len(units) - 1)

            for i in range(TT):
                act.wait_ge(S["wo_mm"], i + 1)
                if i >= 1:
                    act.wait_ge(S["x1_sq"], i)
                a_.activation(ytmp[:, :], bank[:, 2 * (i % 2):2 * (i % 2) + 2, :], ACT.Square,
                              accum_out=stat[:, 40 + i:41 + i]).then_inc(S["wo_sq"], 1)
                act.wait_ge(S["x1_done"], i + 1)
                a_.activation(ytmp[:, :], x1[:, i, :], ACT.Square, accum_out=stat[:, 48 + i:49 + i]).then_inc(S["x1_sq"], 1)
                act.wait_ge(S["h2_done"], i + 1)
                act.dma_start(h_dram[i * P:(i + 1) * P, :], h2[:, i % 2, :]).then_inc(h2_store[i % 2], 16)
                act.wait_ge(S["h2t_mm"], i + 1)
                if i >= 2:
                    act.wait_ge(S["lg_mm"], i - 1)
                a_.activation(h2T[:, i % 2, :, :], bank[:, 4:6, :], ACT.Copy).then_inc(S["h2t_ev"], 1)
            act.wait_ge(S["r_sub"], 1)
            a_.activation(rw("ex"), rw("sub"), ACT.Exp).then_inc(S["r_exp"], 1)

            def take_xT(v):
                for half in range(2):
                    act.wait_ge(S["xtr_done"], 2 * v + half + 1)
                    a_.activation(xT[:, 4 * half:4 * half + 4, :], bank[:, 4 + half, :], ACT.Copy).then_inc(S["xt_ready"], 1)

            def take_aT(v, nb):
                act.wait_ge(S["atr_done"], v + 1)
                a_.activation(aT[:, 0:nb, :, :], bank[:, 4:4 + nb, :], ACT.Copy).then_inc(S["at_ready"], 1)

            def sigmoid(v, nb):
                act.wait_ge(S["g_ready"], v + 1)
                a_.activation(s_sb[:, 0:nb, :], g_sb[:, 0:nb, :], ACT.Sigmoid, scale=ALPHA).then_inc(S["s_ready"], 1)

            def store_y(v, nb, first=False):
                act.wait_ge(S["wout_used"], 4 * (v + 1))
                if not first:
                    act.wait_ge(S["y_stored"], 32 * v)
                a_.activation(y_sb[:, 0:nb, :], bank[:, 6:6 + nb, :], ACT.Copy).then_inc(S["y_evac"], 1)
                act.wait_ge(S["y_evac"], v + 1)
                first_row = act.value_load(row_start[0:1, bass.ds(v, 1)], min_val=0, max_val=T * TOPK)
                rows = y_dram[bass.ds(first_row, nb * BLK), :].rearrange("(b s) n -> s b n", s=BLK)
                for half in range(2):
                    act.dma_start(rows[:, :, half * 512:(half + 1) * 512],
                                  y_sb[64 * half:64 * half + 64, 0:nb, :]).then_inc(S["y_stored"], 16)

            def by_blocks(v, *steps):
                n = act.value_load(flags[0:1, bass.ds(v, 1)], min_val=0, max_val=2)
                with act.If(n > 1):
                    for f in steps:
                        f(2)
                with act.Else():
                    for f in steps:
                        f(1)

            act.wait_ge(S["flags_ready"], 1)
            take_xT(0)
            take_xT(1)
            by_blocks(0, lambda nb: sigmoid(0, nb))
            by_blocks(0, lambda nb: take_aT(0, nb))
            take_xT(2)
            by_blocks(1, lambda nb: sigmoid(1, nb))
            act.wait_ge(S["flags_ready"], 2)
            by_blocks(0, lambda nb: store_y(0, nb, True))
            with act.Fori(2, E) as v:
                by_blocks(v - 1, lambda nb: take_aT(v - 1, nb))
                take_xT(v + 1)
                by_blocks(v, lambda nb: sigmoid(v, nb))
                by_blocks(v - 1, lambda nb: store_y(v - 1, nb))
            by_blocks(E - 1, lambda nb: take_aT(E - 1, nb), lambda nb: store_y(E - 1, nb))
            with act.Fori(0, OVER) as j:
                n = act.value_load(flags[0:1, bass.ds(j + E, 1)], min_val=0, max_val=2)
                with act.If(n > 0):
                    take_xT(j + E + 1)
                    by_blocks(j + E, lambda nb: sigmoid(j + E, nb), lambda nb: take_aT(j + E, nb), lambda nb: store_y(j + E, nb))

            for i in range(TT):
                act.wait_ge(S["yacc"], i + 1)
                a_.activation(region_m[:, i * D:(i + 1) * D], fin_y(i), ACT.Square, accum_out=stat[:, 56 + i:57 + i]).then_inc(S["fin_sq"], 1)
            for i in range(TT):
                act.wait_ge(S["fin_done"], i + 1)
                act.dma_start(out[0, i * P:(i + 1) * P, :], x1[:, i, :]).then_inc(S["out_done"], 16)
            act.wait_ge(S["out_done"], 16 * TT)

        @block.vector
        def _(dve):
            v_ = nc.vector
            step = [0]

            def link(ins):
                step[0] += 1
                ins.then_inc(S["dve_step"], 1)
                dve.wait_ge(S["dve_step"], step[0])

            dve.wait_ge(S["cs_ready"], 1)
            v_.tensor_tensor(crow[:, :], crow[:, :], fwork[0:KT, 0, 0:P], ALU.mult).then_inc(S["csT_done"], 1)
            dve.wait_ge(S["consts"], 1)
            dve.wait_ge(S["vr_done"], 2)
            v_.tensor_copy(vcol[:, :], bank[:, 3, 0:82]).then_inc(S["vcol_ready"], 1)
            v_.tensor_copy(cs_pad[:, :, 0], bank[:, 2, 0:KT]).then_inc(S["csT_ev"], 1)

            def ada_row(n):
                dve.wait_ge(S["ada_mm"], n + 1)
                v_.tensor_copy(mrow[:, n % 2, :], bank[:, ada_bank(n), 0:P]).then_inc(S["ada_row"], 1)

            def ada_col(n):
                dve.wait_ge(S["ada_tr"], n + 1)
                v_.tensor_tensor(modT[:, 4 * n:4 * n + 4], bank[:, ada_bank(n) + 2, 0:P:32], vcol[:, 4 * n:4 * n + 4],
                                 ALU.add).then_inc(S["ada_col"], 1)

            dve.wait_ge(S["vcol_ready"], 1)
            ada_row(0)
            ada_col(0)
            for i in range(TT):
                dve.wait_ge(S["x_sq"], i + 1)
                v_.tensor_scalar(stat[:, 4 + i:5 + i], stat[:, i:i + 1], 1.0 / D, EPS, ALU.mult, ALU.add).then_inc(S["x_ms"], 1)
            for i in range(TT):
                dve.wait_ge(S["x_rstd"], i + 1)
                v_.tensor_scalar(x_sb[:, i, :], x_sb[:, i, :], stat[:, i:i + 1], None, ALU.mult).then_inc(S["x_norm"], 1)
            for n in range(1, 4):
                ada_row(n)
                ada_col(n)
            dve.wait_ge(S["ada_col"], 4)
            v_.scalar_tensor_tensor(ga[:, :], modT[:, 8:16], 1.0, vcol[:, 48:56], ALU.add, ALU.mult).then_inc(S["ga_ready"], 1)
            dve.wait_ge(S["ga_ready"], 1)
            for k in range(0, KT, 2):
                dve.wait_ge(S["xt_mm"], k + 1)
                v_.tensor_scalar(hT[:, k, :], bank[:, 4 + k % 4, :], ga[:, k:k + 1], modT[:, k:k + 1],
                                 ALU.mult, ALU.add).then_inc(S["ht_dve"], 1)

            def gla_operands():
                dve.wait_ge(S["gk_ln"], 1)
                dve.wait_ge(S["consts"], 2)
                for a in range(2):
                    link(v_.tensor_tensor(gtmp[:, a, :], cumT[:, a, :], etmp[:, a, :], ALU.subtract))
                    v_.tensor_tensor_scan(cumT[:, a, :], scan_reset[:, :], gtmp[:, a, :], 0.0, ALU.mult, ALU.add).then_inc(S["cum_done"], 1)
                dve.wait_ge(S["dec_done"], 1)
                wait_out(dve, "qg")
                wait_out(dve, "kg")
                for h in range(GH):
                    r = slice(64 * (h % 2), 64 * (h % 2) + 64)
                    ins = v_.scalar_tensor_tensor(qtp[r, h, :], qg_raw[r, h // 2, :], GK ** -0.5, etmp[r, h // 2, :],
                                                  ALU.mult, ALU.mult)
                link(ins)
                cum = cumT.rearrange("p a (n c) -> p a n c", c=CH)
                for a in range(2):
                    v_.tensor_tensor(etmp[:, a, :].rearrange("p (n c) -> p n c", c=CH),
                                     cum[:, a, :, CH - 1:CH].to_broadcast([P, T // CH, CH]), cum[:, a, :, :],
                                     ALU.subtract).then_inc(S["dd_done"], 1)
                dve.wait_ge(S["enb_done"], 1)
                v_.tensor_tensor(ktT[:, :, :], kg_raw[:, :, :], gtmp[:, :, :], ALU.mult).then_inc(S["gla_ready"], 1)
                dve.wait_ge(S["dk_done"], 1)
                v_.tensor_tensor(kdT[:, :, :], kg_raw[:, :, :], etmp[:, :, :], ALU.mult).then_inc(S["gla_ready"], 1)

            def take_output(j, kind, a, who):
                src = bank[:, j % 4, :]
                if kind == "zf":
                    dve.wait_ge(S["ev_act"], 1)
                    dve.wait_ge(S["fx_in"], 16 * 7)
                    link(v_.tensor_scalar(fwork[32:40, 1, :], zf[32:40, :], bf_col[32:40, :], 0.0, ALU.add, ALU.min))
                    dve.wait_ge(S["fx_ln"], 1)
                    link(v_.tensor_tensor(fwork[32:40, 1, :], fwork[32:40, 1, :], fwork[32:40, 0, :], ALU.subtract))
                    link(v_.memset(fwork[32:40, 0, :], 0.0))
                    v_.tensor_tensor_scan(fwork[32:40, 2, :], fwork[32:40, 1, :], fwork[32:40, 0, :], 0.0, ALU.add, ALU.add).then_inc(S["fx_cum"], 1)
                    dve.wait_ge(S["fx_cum"], 1)
                    v_.tensor_scalar(fwork[32:40, 3, :], fwork[32:40, 2, :], -1.0, None, ALU.mult).then_inc(S["fx_cum"], 1)
                    dve.wait_ge(S["bias_in"], 32)
                    for part in range(2):
                        link(v_.tensor_copy(bias3[:, part, :], bias_raw))
                        link(v_.tensor_tensor(bias_raw, bias_raw, bias3[:, part, :], ALU.subtract))
                    v_.tensor_copy(bias3[:, 2, :], bias_raw).then_inc(S["bias_split"], 1)
                if who != "dve":
                    return
                if kind == "gk":
                    dve.wait_ge(S["gk_abs"], a + 1)
                    dve.wait_ge(S["xt_mm"], KT)
                    v_.tensor_scalar(cumT[:, a, :], src, vcol[:, 80 + a:81 + a], 0.0, ALU.add, ALU.min).then_inc(S["ev_dve"], 1)
                    if a == 1:
                        dve.wait_ge(S["ev_dve"], taken(j)[1])
                        gla_operands()
                elif kind == "gg":
                    dve.wait_ge(S["sig_done"], a + 1)
                    v_.tensor_tensor(gs[:, a, :], src, prob[:, a % 2, :], ALU.mult).then_inc(S["ev_dve"], 1)
                else:
                    dve.wait_ge(S["proj_mm"], j + 1)
                    if kind == "vf":
                        v_.tensor_copy(vf[:, a, :], src).then_inc(S["ev_dve"], 1)
                    else:
                        dst, scale = (ka, 1.0) if kind == "kf" else (qa, FD ** -0.5)
                        dve.wait_ge(S["consts"], 2)
                        v_.tensor_scalar(dst[0:64, 2 * a, :], src[0:64, :], scale, None, ALU.mult)
                        v_.tensor_scalar(dst[0:64, 2 * a + 1, :], src[64:128, :], scale, None, ALU.mult).then_inc(S["ev_dve"], 1)

            for j, (kind, a, who) in enumerate(outs):
                take_output(j, kind, a, who)
                for n in range(4, 10):
                    if ada_behind[n] == j:
                        ada_row(n)
                    if ada_turned[n] == j:
                        ada_col(n)

            for n in (10, 11):
                ada_row(n)
                ada_col(n)
            dve.wait_ge(S["ada_col"], 12)
            v_.tensor_tensor(cols[:, 0, :], modT[:, 16:24], vcol[:, 56:64], ALU.mult)
            v_.scalar_tensor_tensor(cols[:, 1, :], modT[:, 32:40], 1.0, vcol[:, 64:72], ALU.add, ALU.mult)
            v_.tensor_copy(cols[:, 2, :], modT[:, 24:32])
            v_.tensor_tensor(cols[:, 3, :], modT[:, 40:48], vcol[:, 72:80], ALU.mult).then_inc(S["cols_ready"], 1)
            dve.wait_ge(S["cols_ready"], 1)
            dve.wait_ge(S["colT_mm"], 1)
            v_.tensor_copy(mrow[0:32, 0, :], bank[0:32, 7, 0:P]).then_inc(S["vec_ready"], 1)

            def kd_take(i):
                dve.wait_ge(S["kd_mm"], i + 1)
                if i >= 2:
                    dve.wait_ge(S["kv_mm"], 2 * (i - 1))
                for ch in range(2):
                    r = slice(64 * ch, 64 * ch + 64)
                    ins = v_.tensor_copy(kdz[r, i % 2, ch, :], bank[r, 2, 0:256])
                ins.then_inc(S["kd_ev"], 1)

            def st_update(n):
                dve.wait_ge(S["kv_mm"], n + 1)
                if n >= 3:
                    dve.wait_ge(S["go_mm"], (n - 3) // 2 + 1)
                if n:
                    dve.wait_ge(S["st_done"], n)
                else:
                    dve.wait_ge(S["consts"], 3)
                for h in range(GH):
                    r = slice(64 * (h % 2), 64 * (h % 2) + 64)
                    ins = v_.scalar_tensor_tensor(state[r, (n + 1) % 4, h, :], state[r, n % 4, h, :],
                                                  dec[r, h // 2, n:n + 1], bank[r, 3 + n % 2, h * P:(h + 1) * P],
                                                  ALU.mult, ALU.add)
                ins.then_inc(S["st_done"], 1)

            def gla_post(i):
                dve.wait_ge(S["go_ev"], i + 1)
                link(v_.tensor_tensor(osq[:, :], osb[:, :], osb[:, :], ALU.mult))
                ms = stat[:, 24 + 4 * i:28 + 4 * i]
                link(v_.tensor_reduce(ms, osq.rearrange("p (h n) -> p h n", h=GH), AX.X, ALU.add))
                v_.tensor_scalar(ms, ms, 1.0 / GV, EPS, ALU.mult, ALU.add).then_inc(S["go_ms"], 1)
                dve.wait_ge(S["go_rstd"], i + 1)
                rs = stat[:, 8 + 4 * i:12 + 4 * i].rearrange("p (h a) -> p h a", a=1).to_broadcast([P, GH, GV])
                link(v_.tensor_tensor(osq.rearrange("p (h n) -> p h n", h=GH), osb.rearrange("p (h n) -> p h n", h=GH), rs, ALU.mult))
                dve.wait_ge(S["gs_ready"], i + 1)
                v_.tensor_tensor(mix[:, i, 0:512], osq[:, :], gs[:, i, :], ALU.mult).then_inc(S["mixg"], 1)

            kd_take(0)
            for i in range(TT):
                if i + 1 < TT:
                    kd_take(i + 1)
                for n in (2 * i, 2 * i + 1):
                    if n < 7:
                        st_update(n)
                if i >= 1:
                    gla_post(i - 1)

            def fox_max(u):
                qi, h = units[u]
                dve.wait_ge(S["s_done"], u + 1)
                if u >= 4:
                    dve.wait_ge(S["exp_done"], u - 3)
                v_.tensor_reduce(nmax[:, u % 4:u % 4 + 1], bank[:, u % 3, 0:(qi + 1) * P], AX.X, ALU.max,
                                 negate=True).then_inc(S["max_done"], 1)

            def fox_out(qi):
                dve.wait_ge(S["exp_done"], 8 * qi + 8)
                link(v_.reciprocal(rcp[:, :], rsum[:, 8 * qi:8 * qi + 8]))
                dve.wait_ge(S["pv_done"], 8 * qi + 8)
                v_.tensor_tensor(mix[:, qi, 512:1024].rearrange("p (h n) -> p h n", h=FH),
                                 bank[:, 5 + qi % 2, :].rearrange("p (h n) -> p h n", h=FH),
                                 rcp.rearrange("p (h a) -> p h a", a=1).to_broadcast([P, FH, FD]), ALU.mult).then_inc(S["mixf"], 1)

            def mixT_take(qi, half):
                dve.wait_ge(S["mt_mm"], 2 * qi + half + 1)
                v_.tensor_copy(mixT[:, 4 * half:4 * half + 4, qi * P:(qi + 1) * P],
                               bank[:, 7, :].rearrange("p (k t) -> p k t", k=4)).then_inc(S["mt_ev"], 1)

            for w in range(8 * TT + 10):
                if w < len(units):
                    fox_max(w)
                if w == 1:
                    gla_post(TT - 1)
                for qi in range(TT):
                    if w == 8 * qi + 10:
                        fox_out(qi)
                    if w == 8 * qi + 13:
                        mixT_take(qi, 0)
                    if w == 8 * qi + 16:
                        mixT_take(qi, 1)

            def take_logits(i):
                dve.wait_ge(S["lg_mm"], i + 1)
                v_.tensor_tensor(lg[:, i, :], bank[:, 6, i * E:(i + 1) * E], br_bc[:, :], ALU.add).then_inc(S["lg_done"], 1)

            dve.wait_ge(S["x1_in"], 16)
            dve.wait_ge(S["bc_in"], 16 * 3)
            for i in range(TT):
                dve.wait_ge(S["wo_sq"], i + 1)
                v_.tensor_scalar(stat[:, 44 + i:45 + i], stat[:, 40 + i:41 + i], 1.0 / D, EPS, ALU.mult, ALU.add).then_inc(S["wo_ms"], 1)
                dve.wait_ge(S["wo_rstd"], i + 1)
                link(v_.scalar_tensor_tensor(ynorm.rearrange("p (b n) -> p b n", b=2), bank[:, 2 * (i % 2):2 * (i % 2) + 2, :],
                                             stat[:, 40 + i:41 + i], pga.rearrange("p (b n) -> p b n", b=2), ALU.mult, ALU.mult))
                v_.tensor_tensor(x1[:, i, :], x1[:, i, :], ynorm[:, :], ALU.add).then_inc(S["x1_done"], 1)
                dve.wait_ge(S["x1_sq"], i + 1)
                v_.tensor_scalar(stat[:, 52 + i:53 + i], stat[:, 48 + i:49 + i], 1.0 / D, EPS, ALU.mult, ALU.add).then_inc(S["x1_ms"], 1)
                dve.wait_ge(S["x1_rstd"], i + 1)
                if i >= 2:
                    dve.wait_ge(h2_store[i % 2], 16 * (i // 2))
                    dve.wait_ge(S["h2t_mm"], i - 1)
                else:
                    dve.wait_ge(S["mt_mm"], 2 * TT)
                link(v_.scalar_tensor_tensor(h2[:, i % 2, :], x1[:, i, :], stat[:, 48 + i:49 + i], gm[:, :], ALU.mult, ALU.mult))
                v_.tensor_tensor(h2[:, i % 2, :], h2[:, i % 2, :], sm[:, :], ALU.add).then_inc(S["h2_done"], 1)
                if i >= 1:
                    take_logits(i - 1)
            take_logits(TT - 1)
            dve.wait_ge(S["lg_done"], TT)

            top = small[:, 0:32].rearrange("p (i n) -> p i n", i=TT)
            for i in range(TT):
                ins = v_.max(top[:, i, :], lg[:, i, :])
            link(ins)
            shape = [P, TT, E]
            fourth = top[:, :, 3:4].to_broadcast(shape)
            v_.tensor_tensor(rw("sub"), lg[:, :, :], top[:, :, 0:1].to_broadcast(shape), ALU.subtract).then_inc(S["r_sub"], 1)
            v_.tensor_tensor(rw("gt"), lg[:, :, :], fourth, ALU.is_gt)
            link(v_.tensor_tensor(rw("eq"), lg[:, :, :], fourth, ALU.is_equal))
            left = small[:, 32:36]
            v_.tensor_reduce(left, rw("gt"), AX.X, ALU.add)
            flat = lambda n: rw(n).rearrange("p i e -> p (i e)")
            link(v_.tensor_tensor_scan(flat("eqc"), route_reset[:, :], flat("eq"), 0.0, ALU.mult, ALU.add))
            link(v_.tensor_scalar(left, left, -1.0, float(TOPK), ALU.mult, ALU.add))
            link(v_.tensor_tensor(rw("eqc"), rw("eqc"), left.rearrange("p (i a) -> p i a", a=1).to_broadcast(shape), ALU.is_le))
            link(v_.tensor_tensor(rw("eq"), rw("eq"), rw("eqc"), ALU.mult))
            v_.tensor_tensor(rw("mask"), rw("gt"), rw("eq"), ALU.add).then_inc(S["r_mask"], 1)
            dve.wait_ge(S["r_mask"], 1)
            link(v_.tensor_tensor_scan(flat("rk"), route_reset[:, :], flat("mask"), 0.0, ALU.mult, ALU.add))
            link(v_.tensor_tensor(rw("rk"), rw("rk"), rw("mask"), ALU.mult))
            dve.wait_ge(S["r_exp"], 1)
            link(v_.tensor_tensor(rw("ex"), rw("ex"), rw("mask"), ALU.mult))
            link(v_.tensor_reduce(small[:, 36:40], rw("ex"), AX.X, ALU.add))
            link(v_.reciprocal(small[:, 40:44], small[:, 36:40]))
            link(v_.tensor_tensor(rw("gate"), rw("ex"), small[:, 40:44].rearrange("p (i a) -> p i a", a=1).to_broadcast(shape), ALU.mult))
            dve.wait_ge(S["pos_mm"], 2)
            v_.tensor_copy(flat("pos"), bank[:, 7, 0:P])
            cnt, extra, oend, ostart, base = (small[:, 64 + E * n:64 + E * (n + 1)] for n in range(5))
            link(v_.tensor_copy(cnt, bank[:, 5, 0:E]))
            v_.tensor_scalar(flags[0:1, 0:E], cnt[0:1, :], float(BLK), 1.0, ALU.is_gt, ALU.add).then_inc(S["flags_ready"], 1)
            link(v_.tensor_scalar(flat("over"), flat("pos"), float(P), None, ALU.is_ge))
            link(v_.scalar_tensor_tensor(flat("over"), flat("pos"), 2.0 * P, flat("over"), ALU.is_ge, ALU.add))
            link(v_.scalar_tensor_tensor(flat("over"), flat("pos"), 3.0 * P, flat("over"), ALU.is_ge, ALU.add))
            link(v_.tensor_scalar(extra, cnt, float(P), None, ALU.is_gt))
            link(v_.scalar_tensor_tensor(extra, cnt, 2.0 * P, extra, ALU.is_gt, ALU.add))
            link(v_.scalar_tensor_tensor(extra, cnt, 3.0 * P, extra, ALU.is_gt, ALU.add))
            link(v_.tensor_tensor_scan(oend, ones[:, 0:E], extra, 0.0, ALU.mult, ALU.add))
            link(v_.tensor_tensor(ostart, oend, extra, ALU.subtract))
            main, mstart, past, pstart, jump = (small[:, 320 + E * n:320 + E * (n + 1)] for n in range(5))
            link(v_.tensor_scalar(main, cnt, float(P), None, ALU.min))
            link(v_.tensor_tensor_scan(mstart, ones[:, 0:E], main, 0.0, ALU.mult, ALU.add))
            main_rows = small[:, 480:481]
            v_.tensor_copy(main_rows, mstart[:, E - 1:E])
            link(v_.tensor_tensor(past, cnt, main, ALU.subtract))
            link(v_.tensor_tensor(mstart, mstart, main, ALU.subtract))
            v_.tensor_copy(row_start[0:1, 0:E], mstart[0:1, :])
            link(v_.tensor_tensor_scan(pstart, ones[:, 0:E], past, 0.0, ALU.mult, ALU.add))
            link(v_.tensor_tensor(pstart, pstart, past, ALU.subtract))
            link(v_.scalar_tensor_tensor(jump, pstart, main_rows, mstart, ALU.add, ALU.subtract))
            link(v_.tensor_scalar(jump, jump, -float(P), None, ALU.add))
            rows = rw("eqc")
            link(v_.tensor_scalar(rw("eqc"), rw("over"), 0.0, None, ALU.is_gt))
            over_rows = lambda ap: ap.rearrange("p (a e) -> p a e", a=1).to_broadcast(shape)
            link(v_.tensor_tensor(rows, rows, over_rows(jump), ALU.mult))
            link(v_.tensor_tensor(rows, rows, over_rows(mstart), ALU.add))
            link(v_.tensor_tensor(rows, rows, rw("pos"), ALU.add))
            v_.scalar_tensor_tensor(flat("lo"), flat("over"), -float(P), flat("pos"), ALU.mult, ALU.add)
            link(v_.scalar_tensor_tensor(base, ostart, float(E - 1), iota[:, 0:E], ALU.add, ALU.subtract))
            one = lambda ap: ap.rearrange("p (a e) -> p a e", a=1).to_broadcast(shape)
            link(v_.tensor_tensor(rw("vis"), rw("over"), one(base), ALU.add))
            link(v_.scalar_tensor_tensor(flat("vis"), flat("over"), 0.0, flat("vis"), ALU.is_gt, ALU.mult))
            link(v_.tensor_tensor(rw("vis"), rw("vis"), one(iota[:, 0:E]), ALU.add))
            for k in range(TOPK):
                ins = v_.tensor_scalar(sel4[:, :, k, :], rw("rk"), float(k + 1), None, ALU.is_equal)
            link(ins)
            shape4 = [P, TT, TOPK, E]
            lo_k, vis_k = small[:, 224:240], small[:, 240:256]
            row_k = small[:, 304:320]
            for name, dst in (("lo", lo_k), ("vis", vis_k), ("eqc", row_k), ("gate", gate_k[:, :])):
                for i in range(TT):
                    ins = v_.tensor_tensor(prod4[:, i, :, :], sel4[:, i, :, :],
                                           rw(name)[:, i:i + 1, :].to_broadcast([P, TOPK, E]), ALU.mult)
                link(ins)
                link(v_.tensor_reduce(dst.rearrange("p (i k) -> p i k", i=TT), prod4[:, :, :, :], AX.X, ALU.add))
            v_.tensor_copy(slot_k[:, :], row_k)
            dve.wait_ge(S["lg_mm"], TT)
            for q in range(TT * TOPK):
                v_.tensor_scalar(hot_l[:, q, :], iota[:, :], lo_k[:, q:q + 1], None, ALU.is_equal)
                v_.tensor_scalar(hot_v[:, q, :], iota[:, 0:NCOL], vis_k[:, q:q + 1], tid[:, q // TOPK:q // TOPK + 1],
                                 ALU.is_equal, ALU.mult).then_inc(S["hot_ready"], 1)
            dve.wait_ge(S["tab_mm"], 1)
            v_.tensor_copy(tok[:, :], bank[:, 4, 0:NCOL]).then_inc(S["tok_ready"], 1)
            wide = [1, 16, E]
            js = iota[0:1, 0:16].rearrange("p (j a) -> p j a", a=1).to_broadcast(wide)
            row = lambda ap: ap[0:1, :].rearrange("p (a e) -> p a e", a=1).to_broadcast(wide)
            ended, own = (region_h[0:1, 1536 + 512 * n:2048 + 512 * n].rearrange("p (j e) -> p j e", j=16) for n in range(2))
            rest, owns, eo = small[0:1, 256:272], small[0:1, 272:288], small[0:1, 288:304]
            link(v_.tensor_tensor(ended, row(oend), js, ALU.is_le))
            link(v_.tensor_tensor(own, row(ostart), js, ALU.is_le))
            link(v_.tensor_tensor(own, own, ended, ALU.subtract))
            link(v_.tensor_reduce(eo, ended, AX.X, ALU.add))
            link(v_.tensor_reduce(owns, own, AX.X, ALU.add))
            link(v_.scalar_tensor_tensor(base[0:1, :], ostart[0:1, :], float(P), cnt[0:1, :], ALU.mult, ALU.add))
            link(v_.tensor_scalar(base[0:1, :], base[0:1, :], -float(P), None, ALU.add))
            link(v_.tensor_tensor(ended, own, row(base), ALU.mult))
            link(v_.tensor_reduce(rest, ended, AX.X, ALU.add))
            link(v_.tensor_tensor(owns, owns, iota[0:1, 0:16], ALU.mult))
            at = small[0:1, 496:512]
            link(v_.scalar_tensor_tensor(base[0:1, :], ostart[0:1, :], -float(P), pstart[0:1, :], ALU.mult, ALU.add))
            link(v_.tensor_tensor(own, own, row(base), ALU.mult))
            link(v_.tensor_reduce(at, own, AX.X, ALU.add))
            link(v_.scalar_tensor_tensor(at, owns, float(P), at, ALU.mult, ALU.add))
            link(v_.tensor_scalar(row_start[0:1, E:E + 16], at, main_rows[0:1, :], None, ALU.add))
            link(v_.scalar_tensor_tensor(rest, owns, -float(P), rest, ALU.mult, ALU.add))
            link(v_.tensor_copy(over_n[:, :], oend[0:1, E - 1:E]))
            link(v_.tensor_scalar(over_e[:, :], eo, 1.0, None, ALU.mult))
            link(v_.tensor_scalar(eo, rest, 0.0, None, ALU.is_gt))
            v_.scalar_tensor_tensor(flags[0:1, E:E + 16], rest, float(BLK), eo, ALU.is_gt, ALU.add).then_inc(S["flags_ready"], 1)

            def swiglu(v, nb, first=False):
                dve.wait_ge(S["win_used"], 8 * (v + 1))
                v_.tensor_scalar(g_sb[:, 0:nb, :], bank[:, 0:nb, :], LIMIT, None, ALU.min).then_inc(S["g_ready"], 1)
                v_.tensor_scalar(l_sb[:, 0:nb, :], bank[:, 2:2 + nb, :], LIMIT, -LIMIT, ALU.min, ALU.max).then_inc(S["u_free"], 1)
                dve.wait_ge(S["g_ready"], v + 1)
                dve.wait_ge(S["u_free"], v + 1)
                v_.scalar_tensor_tensor(l_sb[:, 0:nb, :], l_sb[:, 0:nb, :], 1.0, g_sb[:, 0:nb, :], ALU.add, ALU.mult).then_inc(S["lin_done"], 1)
                dve.wait_ge(S["lin_done"], v + 1)
                dve.wait_ge(S["s_ready"], v + 1)
                if not first:
                    dve.wait_ge(S["atr_done"], v)
                v_.tensor_tensor(act_a[:, 0:nb, :], l_sb[:, 0:nb, :], s_sb[:, 0:nb, :], ALU.mult).then_inc(S["a_ready"], 1)

            def by_blocks(v, f):
                n = dve.value_load(flags[0:1, bass.ds(v, 1)], min_val=0, max_val=2)
                with dve.If(n > 1):
                    f(2)
                with dve.Else():
                    f(1)

            dve.wait_ge(S["flags_ready"], 2)
            by_blocks(0, lambda nb: swiglu(0, nb, True))
            with dve.Fori(1, E) as v:
                by_blocks(v, lambda nb: swiglu(v, nb))
            with dve.Fori(0, OVER) as j:
                n = dve.value_load(flags[0:1, bass.ds(j + E, 1)], min_val=0, max_val=2)
                with dve.If(n > 0):
                    by_blocks(j + E, lambda nb: swiglu(j + E, nb))

            n = dve.value_load(over_n[0:1, 0:1], min_val=0, max_val=OVER)
            dve.wait_ge(S["wout_used"], 4 * (n + E))
            dve.wait_ge(S["bc_in"], 16 * 4)

            def finish(i):
                dve.wait_ge(S["fin_rstd"], i + 1)
                link(v_.scalar_tensor_tensor(fin_y(i), fin_y(i), stat[:, 56 + i:57 + i], gm[:, :], ALU.mult, ALU.mult))
                v_.tensor_tensor(x1[:, i, :], x1[:, i, :], fin_y(i), ALU.add).then_inc(S["fin_done"], 1)

            def mean_square(i):
                dve.wait_ge(S["fin_sq"], i + 1)
                v_.tensor_scalar(stat[:, 4 + i:5 + i], stat[:, 56 + i:57 + i], 1.0 / D, EPS, ALU.mult, ALU.add).then_inc(S["fin_ms"], 1)

            for i in range(TT):
                dve.wait_ge(fin_in[4 * i], 16)
                link(v_.tensor_scalar(fin_y(i), fin_y(i), gate_k[:, 4 * i:4 * i + 1], None, ALU.mult))
                for k in range(1, TOPK):
                    q = 4 * i + k
                    dve.wait_ge(fin_in[q], 16)
                    ins = v_.scalar_tensor_tensor(fin_y(i), row_buf(q), gate_k[:, q:q + 1], fin_y(i), ALU.mult, ALU.add)
                    if k < TOPK - 1:
                        link(ins)
                    else:
                        ins.then_inc(S["yacc"], 1)
                if i >= 1:
                    mean_square(i - 1)
                    finish(i - 1)
            mean_square(TT - 1)
            finish(TT - 1)

        @block.tensor
        def _(pe):
            t_ = nc.tensor

            def turn(dst, src, n=P):
                return t_.transpose(dst, src, ident[0:n, 0:n])

            pe.wait_ge(S["small_in"], 16 * 6)
            pe.wait_ge(S["consts"], 1)
            turn(bank[:, 3, 0:82], vrows[:, :], 82).then_inc(S["vr_done"], 1)
            pe.wait_ge(S["csT_done"], 1)
            turn(bank[:, 2, 0:KT], crow[:, :], KT).then_inc(S["vr_done"], 1)
            pe.wait_ge(S["csT_ev"], 1)

            def ada_rows(n):
                s = at_chunk[("ada", n)]
                pe.wait_ge(stream[s % 3], 16 * (s // 3 + 1))
                if n >= 2:
                    pe.wait_ge(S["ada_row"], n - 1)
                w = chunk_buf(s)
                for k in range(KT):
                    for q in range(4):
                        ins = t_.matmul(bank[32 * q:32 * q + 32, ada_bank(n), 0:P], lhsT=cs_pad[:, k, :], rhs=w[:, k, q * P:(q + 1) * P],
                                        start=(k == 0), stop=(k == KT - 1), tile_position=(0, 32 * q))
                ins.then_inc(S["ada_mm"], 1)

            def ada_turn(n):
                pe.wait_ge(S["ada_row"], n + 1)
                if n >= 2:
                    pe.wait_ge(S["ada_col"], n - 1)
                turn(bank[:, ada_bank(n) + 2, 0:P], mrow[:, n % 2, :]).then_inc(S["ada_tr"], 1)

            for n in range(4):
                ada_rows(n)
                ada_turn(n)
            pe.wait_ge(S["x_norm"], TT)
            for k in range(KT):
                if k >= 4:
                    pe.wait_ge(S["ht_act"] if k % 2 else S["ht_dve"], (k - 4) // 2 + 1)
                for i in range(TT):
                    ins = turn(bank[:, 4 + k % 4, i * P:(i + 1) * P], x_sb[:, i, k * P:(k + 1) * P])
                ins.then_inc(S["xt_mm"], 1)
            pe.wait_ge(S["ht_act"], 4)
            pe.wait_ge(S["ht_dve"], 4)
            pe.wait_ge(S["ada_col"], 4)
            pe.wait_ge(S["fx_in"], 16 * 7)

            for j, (kind, a, who) in enumerate(outs):
                if j >= 4:
                    pe.wait_ge(*taken(j - 4))
                base = {"qg": C_QG, "kg": C_QG, "gg": C_GG, "vg": C_VG, "kf": C_KF, "qf": C_QF, "vf": C_VF}.get(kind)
                if base is not None:
                    s = at_chunk[("in", base)]
                    pe.wait_ge(stream[s % 3], 16 * (s // 3 + 1))
                    w = chunk_buf(s)
                if kind == "gk":
                    pe.wait_ge(*taken(out_at[("zf", 0)]))
                    ins = t_.matmul(bank[:, j % 4, :], lhsT=wgk[:, a * P:(a + 1) * P], rhs=zf[0:LR, :], start=True, stop=True)
                for k in range(KT if kind != "gk" else 0):
                    if kind == "zf":
                        dst, lhsT, rhs = bank[0:40, j % 4, :], wzf[:, k, :], hT[:, k, :]
                    elif kind in ("qg", "kg", "kf", "qf"):
                        at = a * P + (256 if kind == "kg" else 0)
                        dst, lhsT, rhs = bank[:, j % 4, :], w[:, k, at:at + P], hT[:, k, :]
                    else:
                        dst, lhsT, rhs = bank[:, j % 4, :], hT[:, k, a * P:(a + 1) * P], w[:, k, :]
                    ins = t_.matmul(dst, lhsT=lhsT, rhs=rhs, start=(k == 0), stop=(k == KT - 1))
                ins.then_inc(S["proj_mm"], 1)
                for n in range(4, 10):
                    if ada_behind[n] == j:
                        ada_rows(n)
                    if ada_turned[n] == j:
                        ada_turn(n)
            for n in (10, 11):
                ada_rows(n)
                ada_turn(n)
            for back in range(4):
                pe.wait_ge(*taken(len(outs) - 1 - back))

            pe.wait_ge(S["gla_ready"], 2)
            pe.wait_ge(S["ada_col"], 12)
            wait_out(pe, "vg")

            def gla_scores(i):
                cols_ = slice(i * P, (i + 1) * P)
                if i >= 1:
                    pe.wait_ge(S["kd_ev"], i)
                for a in range(2):
                    ins = turn(bank[:, 2, a * P:(a + 1) * P], kdT[:, a, cols_])
                ins.then_inc(S["kd_mm"], 1)
                if i >= 2:
                    pe.wait_ge(S["att_cp"], i - 1)
                for h in range(GH):
                    ins = t_.matmul(bank[:, i % 2, h * P:(h + 1) * P], lhsT=ktT[:, h // 2, cols_], rhs=qtp[:, h, cols_],
                                    start=True, stop=True)
                ins.then_inc(S["att_mm"], 1)

            def gla_out(i):
                pe.wait_ge(S["kd_ev"], i + 1)
                if i == 0:
                    pe.wait_ge(S["consts"], 3)
                else:
                    pe.wait_ge(S["st_done"], 2 * i)
                for ch in range(2 if i < TT - 1 else 1):
                    for a in range(2):
                        ins = t_.matmul(bank[:, 3 + ch, a * 256:(a + 1) * 256], lhsT=kdz[:, i % 2, ch, a * P:(a + 1) * P],
                                        rhs=vg[:, i, a * 256:(a + 1) * 256], start=True, stop=True)
                    ins.then_inc(S["kv_mm"], 1)
                pe.wait_ge(S["att_ready"], i + 1)
                if i >= 2:
                    pe.wait_ge(S["go_ev"], i - 1)
                pe.wait_ge(S["st_done"], 2 * i + 1)
                ob = bank[:, 5 + i % 2, :]
                for h in range(GH):
                    hs = slice(h * P, (h + 1) * P)
                    t_.matmul(ob[:, hs], lhsT=attz[:, i % 2, h, :], rhs=vg[:, i, hs], start=True, stop=False, skip_group_check=True)
                    for ch in range(2):
                        r = slice(64 * ch, 64 * ch + 64)
                        ins = t_.matmul(ob[r, hs], lhsT=qtp[:, h, i * P + 64 * ch:i * P + 64 * ch + 64],
                                        rhs=state[:, (2 * i + ch) % 4, h, :], start=False, stop=True, skip_group_check=True)
                ins.then_inc(S["go_mm"], 1)

            gla_scores(0)
            pe.wait_ge(S["cols_ready"], 1)
            turn(bank[0:32, 7, 0:P], cols[:, :, :].rearrange("p a k -> p (a k)")).then_inc(S["colT_mm"], 1)
            for i in range(TT):
                if i + 1 < TT:
                    gla_scores(i + 1)
                gla_out(i)

            pe.wait_ge(S["fx_in"], 16 * 9)
            wait_out(pe, "kf")
            wait_out(pe, "qf")
            wait_out(pe, "vf")
            pe.wait_ge(S["consts"], 2)

            def fox_scores(u):
                qi, h = units[u]
                if u >= 3:
                    pe.wait_ge(S["exp_done"], u - 2)
                elif u == 0:
                    pe.wait_ge(S["att_cp"], TT)
                    pe.wait_ge(S["kd_ev"], TT)
                n = (qi + 1) * P
                t_.matmul(bank[:, u % 3, 0:n], lhsT=qa[:, h, qi * P:n], rhs=ka[:, h, 0:n], start=True, stop=False, skip_group_check=True)
                t_.matmul(bank[:, u % 3, qi * P:n], lhsT=identb[:, :], rhs=maskb[:, :], start=False, stop=True,
                          skip_group_check=True).then_inc(S["s_done"], 1)

            def fox_turn(u):
                qi, h = units[u]
                pe.wait_ge(S["exp_done"], u + 1)
                if u >= 2:
                    pe.wait_ge(S["pt_ev"], u - 1)
                else:
                    pe.wait_ge(S["st_done"], 7)
                for kb in range(qi + 1):
                    ins = turn(bank[:, 3 + u % 2, kb * P:(kb + 1) * P], prob[:, u % 2, kb * P:(kb + 1) * P])
                ins.then_inc(S["pt_done"], 1)

            def fox_values(u):
                qi, h = units[u]
                pe.wait_ge(S["pt_ev"], u + 1)
                if h == 0:
                    if qi >= 2:
                        pe.wait_ge(S["mixf"], qi - 1)
                    else:
                        pe.wait_ge(S["go_ev"], 3 + qi)
                for kb in range(qi + 1):
                    ins = t_.matmul(bank[:, 5 + qi % 2, h * FD:(h + 1) * FD], lhsT=probT[:, u % 2, kb * P:(kb + 1) * P],
                                    rhs=vf[:, kb, h * FD:(h + 1) * FD], start=(kb == 0), stop=(kb == qi))
                ins.then_inc(S["pv_done"], 1)

            def mix_turn(qi, half):
                pe.wait_ge(S["mixg"], qi + 1)
                pe.wait_ge(S["mixf"], qi + 1)
                if qi + half:
                    pe.wait_ge(S["mt_ev"], 2 * qi + half)
                else:
                    pe.wait_ge(S["vec_ready"], 1)
                for k in range(4):
                    ins = turn(bank[:, 7, k * P:(k + 1) * P], mix[:, qi, (4 * half + k) * P:(4 * half + k + 1) * P])
                ins.then_inc(S["mt_mm"], 1)

            for w in range(8 * TT + 10):
                if w < len(units):
                    fox_scores(w)
                if 1 <= w <= len(units):
                    fox_turn(w - 1)
                if 2 <= w <= len(units) + 1:
                    fox_values(w - 2)
                for qi in range(TT):
                    for half in range(2):
                        if w == 8 * qi + 12 + 3 * half:
                            mix_turn(qi, half)
            for half in range(2):
                if 8 * (TT - 1) + 12 + 3 * half >= 8 * TT + 10:
                    mix_turn(TT - 1, half)

            pe.wait_ge(S["wo_in"], 16)

            def project(i):
                pe.wait_ge(S["mt_ev"], 2 * TT)
                if i >= 2:
                    pe.wait_ge(S["x1_done"], i - 1)
                elif i == 0:
                    pe.wait_ge(S["exp_done"], len(units))
                    pe.wait_ge(S["pt_ev"], len(units))
                for n in range(2):
                    for k in range(KT):
                        ins = t_.matmul(bank[:, 2 * (i % 2) + n, :], lhsT=mixT[:, k, i * P:(i + 1) * P],
                                        rhs=wo_sb[:, k, n * 512:(n + 1) * 512], start=(k == 0), stop=(k == KT - 1))
                ins.then_inc(S["wo_mm"], 1)

            def logits(i):
                pe.wait_ge(S["h2_done"], i + 1)
                if i >= 1:
                    pe.wait_ge(S["h2t_ev"], i)
                for k in range(KT):
                    ins = turn(bank[:, 4 + k // 4, (k % 4) * P:(k % 4 + 1) * P], h2[:, i % 2, k * P:(k + 1) * P])
                ins.then_inc(S["h2t_mm"], 1)
                pe.wait_ge(S["h2t_ev"], i + 1)
                if i >= 1:
                    pe.wait_ge(S["lg_done"], i)
                for k in range(KT):
                    ins = t_.matmul(bank[:, 6, i * E:(i + 1) * E], lhsT=h2T[:, i % 2, k, :], rhs=w_r[:, k, :],
                                    start=(k == 0), stop=(k == KT - 1))
                ins.then_inc(S["lg_mm"], 1)

            for i in range(TT):
                project(i)
                if i >= 1:
                    logits(i - 1)
            logits(TT - 1)

            pe.wait_ge(S["r_mask"], 1)
            for i in range(TT):
                for j in range(i + 1):
                    ins = t_.matmul(bank[:, 7, i * E:(i + 1) * E], lhsT=before[:, :] if j == i else ones[:, :], rhs=rw("mask")[:, j, :],
                                    start=(j == 0), stop=(j == i))
            ins.then_inc(S["pos_mm"], 1)
            for j in range(TT):
                ins = t_.matmul(bank[:, 5, 0:E], lhsT=ones[:, :], rhs=rw("mask")[:, j, :], start=(j == 0), stop=(j == TT - 1))
            ins.then_inc(S["pos_mm"], 1)
            for q in range(TT * TOPK):
                pe.wait_ge(S["hot_ready"], q + 1)
                ins = t_.matmul(bank[:, 4, 0:NCOL], lhsT=hot_l[:, q, :], rhs=hot_v[:, q, :], start=(q == 0), stop=(q == TT * TOPK - 1))
            ins.then_inc(S["tab_mm"], 1)

            def turn_x(v, first=False):
                pe.wait_ge(S["gathered"], 16 * (v + 1))
                if not first:
                    pe.wait_ge(S["at_ready"], v - 1)
                for k in range(KT):
                    ins = turn(bank[:, 4 + k // 4, (k % 4) * P:(k % 4 + 1) * P], xg[:, k * P:(k + 1) * P])
                    if k % 4 == 3:
                        ins.then_inc(S["xtr_done"], 1)

            def up(v, nb, first=False):
                pe.wait_ge(S["xt_ready"], 2 * v + 2)
                pe.wait_ge(S["up_bias_in"], 16 * (v + 1))
                if not first:
                    pe.wait_ge(S["u_free"], v)
                for b in range(nb):
                    for g in range(2):
                        for half in range(2):
                            ins = t_.matmul(bank[64 * half:64 * half + 64, 2 * g + b, :], lhsT=ones3[:, :],
                                            rhs=bup[:, g * D + half * 512:g * D + half * 512 + 512], start=True, stop=False,
                                            tile_position=(0, 64 * half), skip_group_check=True)
                ins.then_inc(S["up_bias_used"], 1)
                for k in range(KT):
                    pe.wait_ge(w_slot[k], 16 * (v + 1))
                    for b in range(nb):
                        for g in range(2):
                            for half in range(2):
                                ins = t_.matmul(bank[64 * half:64 * half + 64, 2 * g + b, :],
                                                lhsT=xT[:, k, BLK * b:BLK * b + BLK],
                                                rhs=slot(k)[:, g * D + half * 512:g * D + half * 512 + 512],
                                                start=False, stop=(k == KT - 1), tile_position=(0, 64 * half), skip_group_check=True)
                    ins.then_inc(S["win_used"], 1)

            def turn_a(v, nb):
                pe.wait_ge(S["a_ready"], v + 1)
                pe.wait_ge(S["xt_ready"], 2 * v + 4)
                for b in range(nb):
                    for q in range(4):
                        ins = turn(bank[:, 4 + b, q * P:(q + 1) * P], act_a[:, b, q * P:(q + 1) * P])
                ins.then_inc(S["atr_done"], 1)

            def down(v, nb, first=False):
                pe.wait_ge(S["at_ready"], v + 1)
                pe.wait_ge(S["dn_bias_in"], 16 * (v + 1))
                if not first:
                    pe.wait_ge(S["y_evac"], v)
                for b in range(nb):
                    for half in range(2):
                        ins = t_.matmul(bank[64 * half:64 * half + 64, 6 + b, :], lhsT=ones3[:, :],
                                        rhs=bdn[:, half * 512:half * 512 + 512], start=True, stop=False,
                                        tile_position=(0, 64 * half), skip_group_check=True)
                ins.then_inc(S["dn_bias_used"], 1)
                for j in range(4):
                    pe.wait_ge(w_slot[8 + j], 16 * (v + 1))
                    for kk in range(2):
                        kt = 2 * j + kk
                        for b in range(nb):
                            for half in range(2):
                                ins = t_.matmul(bank[64 * half:64 * half + 64, 6 + b, :],
                                                lhsT=aT[:, b, kt % 4, BLK * (kt // 4):BLK * (kt // 4) + BLK],
                                                rhs=slot(8 + j)[:, kk * D + half * 512:kk * D + half * 512 + 512],
                                                start=False, stop=(kt == KT - 1), tile_position=(0, 64 * half), skip_group_check=True)
                    ins.then_inc(S["wout_used"], 1)

            def by_blocks(v, f):
                n = pe.value_load(flags[0:1, bass.ds(v, 1)], min_val=0, max_val=2)
                with pe.If(n > 1):
                    f(2)
                with pe.Else():
                    f(1)

            pe.wait_ge(S["flags_ready"], 2)
            turn_x(0, True)
            by_blocks(0, lambda nb: up(0, nb, True))
            pe.wait_ge(S["xt_ready"], 2)
            turn_x(1, True)
            by_blocks(0, lambda nb: turn_a(0, nb))
            by_blocks(1, lambda nb: up(1, nb))
            turn_x(2)
            by_blocks(0, lambda nb: down(0, nb, True))
            with pe.Fori(2, E) as v:
                by_blocks(v - 1, lambda nb: turn_a(v - 1, nb))
                by_blocks(v, lambda nb: up(v, nb))
                turn_x(v + 1)
                by_blocks(v - 1, lambda nb: down(v - 1, nb))
            by_blocks(E - 1, lambda nb: (turn_a(E - 1, nb), down(E - 1, nb)))
            with pe.Fori(0, OVER) as j:
                n = pe.value_load(flags[0:1, bass.ds(j + E, 1)], min_val=0, max_val=2)
                with pe.If(n > 0):
                    by_blocks(j + E, lambda nb: up(j + E, nb))
                    turn_x(j + E + 1)
                    by_blocks(j + E, lambda nb: (turn_a(j + E, nb), down(j + E, nb)))


_INS = ['x', 'c', 'w_ada', 'b_ada', 'attn_pre_gain', 'attn_post_gain', 'w_in', 'w_gk2', 'b_gk', 'gla_norm_gain',
        'b_f', 'w_o', 'mlp_pre_gain', 'mlp_post_gain', 'w_router', 'b_router', 'w_e_in', 'b_e_in', 'w_e_out', 'b_e_out']


def kernel(**inputs):
    import numpy as _np
    import concourse.bacc as _bacc
    from concourse import mybir as _mybir
    from concourse.bass_utils import run_bass_kernel_spmd as _run

    nc = _bacc.Bacc("TRN2", target_bir_lowering=False, num_devices=1)
    arrays, args = {}, []
    for name in _INS:
        a = _np.ascontiguousarray(inputs[name])
        arrays[f"in_{name}_dram"] = a
        args.append(nc.dram_tensor(f"in_{name}_dram", a.shape, _mybir.dt.from_np(a.dtype), kind="ExternalInput").ap())
    out = nc.dram_tensor("out_0_dram", (1, T, D), _mybir.dt.float32, kind="ExternalOutput").ap()
    build(nc, *args, out)
    r = _run(nc, [arrays], core_ids=[0])
    return r.results[0]["out_0_dram"]
```

```python
from contextlib import ExitStack

import concourse.bass as bass
from concourse import mybir

F32 = mybir.dt.float32
BF16 = mybir.dt.bfloat16
I32 = mybir.dt.int32
ALU = mybir.AluOpType
ACT = mybir.ActivationFunctionType
AX = mybir.AxisListType

P = 128
D = 1024
KT = D // P
T = 512
TT = T // P
EPS = 1e-6
GH, GK, GV, CH = 4, 64, 128, 64
FH, FD = 8, 64
GLA_NORM = 16.0
LR = 16
C_QG, C_KG, C_VG, C_GG, C_Z, C_QF, C_KF, C_VF, C_FF = 0, 256, 512, 1024, 1536, 1552, 2064, 2576, 3088
E = 32
TOPK = 4
ALPHA, LIMIT = 1.702, 7.0
BLK = 64
EXTRA = T * TOPK // P - 1
GROUPS, PAIRS = 4, 2
NV = E + GROUPS * PAIRS * 2
assert NV >= E + EXTRA
NCOL = NV + 2
SLOT = 2048
NEG = -1.0e30


def build(nc, x, c, w_ada, b_ada, attn_pre_gain, attn_post_gain, w_in, w_gk2, b_gk, gla_norm_gain,
          b_f, w_o, mlp_pre_gain, mlp_post_gain, w_router, b_router, w_e_in, b_e_in, w_e_out,
          b_e_out, out):
    h_dram = nc.dram_tensor("h_rows", (T, D), F32).ap()
    acc_dram = [nc.dram_tensor(f"expert_sums{b}", (P + 2 * T, 512), F32).ap() for b in range(2)]
    vec_dram = nc.dram_tensor("norm_vectors", (4, D), F32).ap()
    bias_dram = nc.dram_tensor("bias_parts", (E, 3, 3 * D), BF16).ap()

    with ExitStack() as ctx:
        def sb(name, shape, dt=F32):
            return ctx.enter_context(nc.sbuf_tensor(name, shape, dt))

        def sem(name):
            return ctx.enter_context(nc.semaphore(name))

        ring = sb("ring", [P, 12 * SLOT])
        region_x = sb("region_x", [P, TT * D])
        region_h = sb("region_h", [P, TT * D])
        region_1 = sb("region_1", [P, TT * D])
        region_m = sb("region_m", [P, 8192])
        bank = ctx.enter_context(nc.psum_tensor("bank", [P, 8, 512], F32))

        def chunk_buf(s):
            return ring[:, (s % 3) * 2 * SLOT:(s % 3 + 1) * 2 * SLOT].rearrange("p (k n) -> p k n", k=KT)

        def slot(j):
            return ring[:, j * SLOT:(j + 1) * SLOT]

        qa = ring[0:66, 6 * SLOT:8 * SLOT].rearrange("p (h t) -> p h t", h=FH)
        ka = ring[0:66, 8 * SLOT:10 * SLOT].rearrange("p (h t) -> p h t", h=FH)
        vf = slot(10).rearrange("p (i n) -> p i n", i=TT)
        vg = slot(11).rearrange("p (i n) -> p i n", i=TT)
        wo_sb = ring[:, 0:4 * SLOT].rearrange("p (k n) -> p k n", k=KT)

        x_sb = region_x[:, :].rearrange("p (i n) -> p i n", i=TT)
        qg_raw = region_x[:, 0:1024].rearrange("p (a t) -> p a t", a=2)
        kg_raw = region_x[:, 1024:2048].rearrange("p (a t) -> p a t", a=2)
        cumT = region_x[:, 2048:3072].rearrange("p (a t) -> p a t", a=2)
        gtmp = region_x[:, 3072:4096].rearrange("p (a t) -> p a t", a=2)
        mix = x_sb
        h2 = region_x[:, 0:2048].rearrange("p (b n) -> p b n", b=2)
        h2T = region_x[:, 2048:4096].rearrange("p (b k t) -> p b k t", b=2, k=KT)
        bias3 = ring[0:E, 6 * SLOT:6 * SLOT + 9 * D // 2].bitcast(BF16).rearrange("p (j n) -> p j n", j=3)
        hT = region_h[:, :].rearrange("p (k t) -> p k t", k=KT)
        mixT = hT
        bias_raw = region_1[0:E, 0:3 * D]
        prob = region_1[:, 0:1024].rearrange("p (b n) -> p b n", b=2)
        probs = [region_1[:, 0:512], region_1[:, 512:1024], region_1[:, 2048:2560]]
        probT = region_1[:, 1024:2048].rearrange("p (b n) -> p b n", b=2)
        attz = region_1[:, 2048:3072].rearrange("p (b h n) -> p b h n", b=2, h=GH)
        osb = region_1[:, 3072:3584]
        osq = region_1[:, 3584:4096]
        zf = region_1[0:40, 3072:3584]
        x1 = region_1[:, :].rearrange("p (i n) -> p i n", i=TT)
        gs = region_m[:, 0:2048].rearrange("p (i n) -> p i n", i=TT)
        qtp = region_m[:, 2048:4096].rearrange("p (h t) -> p h t", h=GH)
        ktT = region_m[:, 4096:5120].rearrange("p (a t) -> p a t", a=2)
        kdT = region_m[:, 5120:6144].rearrange("p (a t) -> p a t", a=2)
        etmp = region_m[:, 6144:7168].rearrange("p (a t) -> p a t", a=2)
        kdz = region_m[:, 7168:8192].rearrange("p (b c n) -> p b c n", b=2, c=2)
        ytmp = region_m[:, 2048:3072]
        ynorm = region_m[:, 3072:4096]
        xg = [region_m[:, 0:1024], region_x[:, 0:1024]]
        xT = region_m[:, 1024:2048].rearrange("p (k s) -> p k s", k=KT)
        act_a = region_m[:, 2048:3072].rearrange("p (b n) -> p b n", b=2)
        aT = region_m[:, 3072:4096].rearrange("p (b c s) -> p b c s", b=2, c=4)
        y_sb = [buf.rearrange("p (b n) -> p b n", b=2) for buf in (region_m[:, 4096:5120], region_x[:, 1024:2048])]
        g_sb = region_m[:, 5120:6144].rearrange("p (b n) -> p b n", b=2)
        s_sb = region_m[:, 6144:7168].rearrange("p (b n) -> p b n", b=2)
        l_sb = region_m[:, 7168:8192].rearrange("p (b n) -> p b n", b=2)

        state = sb("state", [P, 4, GH, GV])
        pga = sb("pga", [P, D])
        gm = sb("gm", [P, D])
        sm = sb("sm", [P, D])
        ident = sb("ident", [P, P])
        ones = sb("ones", [P, P], BF16)
        before = sb("before", [P, P], BF16)
        iota = sb("iota", [P, P])
        identb = sb("identb", [P, P], BF16)
        maskb = sb("maskb", [P, P], BF16)
        ones3 = sb("ones3", [3, BLK], BF16)
        tid = sb("tid", [P, TT])
        scan_reset = sb("scan_reset", [P, T], BF16)
        route_reset = sb("route_reset", [P, P], BF16)
        half_pow = sb("half_pow", [P, 4])
        cs_flat = sb("cs_flat", [P, KT * 32])
        cs_pad = cs_flat[:, :].rearrange("p (k n) -> p k n", k=KT)
        crow = region_m[0:KT, 448:576]
        vrows = region_m[0:82, 320:448]
        vcol = sb("vcol", [P, 82])
        modT = sb("modT", [P, 48])
        ga = sb("ga", [P, KT])
        cols = sb("cols", [P, 4, KT])
        mrow = sb("mrow", [P, 2, P])
        gain_bc = sb("gain_bc", [P, T])
        br_bc = sb("br_bc", [P, E])
        wzf = region_m[:, 0:320].rearrange("p (k n) -> p k n", k=KT)
        wgk = region_1[0:LR, 3584:3840]
        bf_col = sb("bf_col", [40, 1])
        fwork = state[0:40, :, :, :].rearrange("p a h v -> p a (h v)")
        w_r = sb("w_r", [P, KT, E])
        stat = sb("stat", [P, 64])
        rsum = sb("rsum", [P, 32])
        nmax = sb("nmax", [P, 4])
        dec = sb("dec", [P, 2, T // CH])
        lg = sb("lg", [P, TT, E])
        gate_col = cs_flat[:, 0:2 * NCOL]
        row_col = cs_flat[:, 2 * NCOL:4 * NCOL].bitcast(I32)
        row_now = sb("row_now", [P, 2], I32)
        tok = sb("tok", [P, NCOL], I32)
        tok_now = sb("tok_now", [P, 2], I32)
        visits = sb("visits", [1, 4, NCOL], I32)
        bup = state[0:3, 0:2, :, :].rearrange("p a h v -> p (a h v)").bitcast(BF16)
        bdn = state[0:3, 2:3, :, :].rearrange("p a h v -> p (a h v)").bitcast(BF16)
        rcp = sb("rcp", [P, FH])
        word = sb("word", [1, 1])
        mark = sb("mark", [P, 4])

        WORK = "sub ex eq eqc gt mask rk code gate".split()

        def rw(name):
            j = WORK.index(name)
            return region_h[:, j * P:(j + 1) * P].rearrange("p (i e) -> p i e", i=TT)

        sel4 = region_h[:, 1536:2048].rearrange("p (i k e) -> p i k e", i=TT, k=TOPK)
        prod4 = region_h[:, 2048:2560].rearrange("p (i k e) -> p i k e", i=TT, k=TOPK)
        hot_v = region_h[:, 2528:2528 + 16 * NCOL].bitcast(BF16).rearrange("p (q n) -> p q n", q=16)
        small = region_h[:, 3328:4096]
        lo_k, vis_k = small[:, 544 + 32:544 + 48], small[:, 544 + 48:544 + 64]
        hot_l = region_x[:, 2048:3072].bitcast(BF16).rearrange("p (q n) -> p q n", q=16)

        mask_bf = small[:, 512:576].bitcast(BF16)
        first_rhs = small[0:E, 608:624].bitcast(BF16)
        hot2_l = region_x[:, 2048:4096].rearrange("p (q h n) -> p q h n", q=16, h=2)
        hot2_v = region_h[:, 0:16 * 4 * NCOL].rearrange("p (q n) -> p q n", q=16)

        def fin_y(i):
            return ring[:, i * D:(i + 1) * D]

        def fin_z(i):
            return ring[:, (2 * TT + i) * D:(2 * TT + i + 1) * D]

        def fin_t(i):
            return ring[:, (TT + i) * D:(TT + i + 1) * D]

        names = """consts small_in crow_in x_in stream0 stream1 stream2 vr_done
            vcol_ready cs_ready csT_done csT_ev ada_mm ada_row ada_tr ada_col x_sq x_rstd x_norm xt_mm
            ga_ready ht_act ht_dve proj_mm ev_act ev_dve sig_done dve_step act_step pool_step
            fx_ln fx_cum fx_in gk_abs gk_ln cum_done enb_done dd_done dk_done
            dec_done gla_ready gs_ready bias_in bias_split bias_out cols_ready colT_mm vec_ready vec_out bc_in 
            kd_mm kd_ev att_mm att_cp att_ready kv_mm st_done go_mm go_ev go_ms go_rstd mixg
            s_done max_done exp_done pt_done pt_ev pv_done mixf mt_mm mt_ev wo_in x1_in wo_mm wo_sq wo_rstd
            x1_done x1_sq x1_rstd h2_done h2_store0 h2_store1 gathered0 gathered1 h2t_mm h2t_ev lg_mm lg_done r_sub r_exp r_mask pos_mm
            hot_ready tab_mm tok_ready
            up_bias_in dn_bias_in up_bias_used dn_bias_used win_used wout_used tok_copied xtr_done
            xt_ready u_free g_ready s_ready a_ready atr_done at_ready y_evac 
            fin_sq fin_rstd fin_done out_done lin_done acc_zero visits_ready col_ready hot2_ready tab2_mm sel_ready visit_cols visit_mm row_copied norm_done yacc first_ready first_mm""".split()
        S = {n: sem(n) for n in names}
        fin_in = [sem(f"fin_in{i}") for i in range(TT)]
        scattered = [sem(f"scattered{b}") for b in range(2)]
        w_slot = [sem(f"w_slot{j}") for j in range(12)]
        gathered = [S["gathered0"], S["gathered1"]]
        h2_store = [S["h2_store0"], S["h2_store1"]]
        stream = [S["stream0"], S["stream1"], S["stream2"]]

        PROJ = [C_QG, C_GG, C_VG, C_KF, C_QF, C_VF]
        chunks = [("ada", n) for n in range(4)]
        ADA_AFTER = [(4,), (5, 6), (7,), (8, 9), (10,), (11,)]
        for at, ns in zip(PROJ, ADA_AFTER):
            chunks += [("in", at)] + [("ada", n) for n in ns]
        at_chunk = {ch: s for s, ch in enumerate(chunks)}

        outs = [("zf", 0, "act")]
        outs += [("qg", a, "act") for a in range(2)] + [("kg", a, "act") for a in range(2)]
        outs += [("gk", a, "dve") for a in range(2)]
        outs += [("gg", i, "dve") for i in range(TT)] + [("vg", i, "act") for i in range(TT)]
        outs += [("kf", a, "act" if a % 2 else "dve") for a in range(4)]
        outs += [("qf", a, "act" if a % 2 else "dve") for a in range(4)]
        outs += [("vf", i, "act" if i % 2 else "dve") for i in range(TT)]
        out_at = {(k, a): j for j, (k, a, _) in enumerate(outs)}

        lasts = [("kg", 1), ("gg", 3), ("vg", 3), ("kf", 3), ("qf", 3), ("vf", 3)]
        ada_behind = {n: out_at[last] for last, ns in zip(lasts, ADA_AFTER) for n in ns}
        ada_turned = {n: min(j + 2, len(outs) - 1) for n, j in ada_behind.items()}

        def ada_bank(n):
            return n % 2 + (4 if n >= 4 else 0)

        def taken(j):
            who = outs[j][2]
            return S["ev_" + who], sum(1 for o in outs[:j + 1] if o[2] == who)

        def wait_out(eng, kind):
            for who in ("act", "dve"):
                js = [j for j, o in enumerate(outs) if o[0] == kind and o[2] == who]
                if js:
                    eng.wait_ge(*taken(js[-1]))

        def wait_used(eng, s):
            kind, n = chunks[s]
            if kind == "ada":
                eng.wait_ge(S["ada_mm"], n + 1)
            else:
                eng.wait_ge(S["proj_mm"], out_at[lasts[PROJ.index(n)]] + 1)

        def acc_rows(i, b):
            return acc_dram[b][P + 2 * P * i:P + 2 * P * (i + 1), :].rearrange("(p h) n -> p (h n)", h=2)

        units = [(qi, h) for qi in range(TT) for h in range(FH)]
        block = ctx.enter_context(nc.Block())

        @block.sync
        def _(sp):
            sp.dma_start(crow[:, :], c.rearrange("b (k p) -> (b k) p", p=P)).then_inc(S["crow_in"], 16)
            vectors = [
                (vrows[0:48, :], b_ada.rearrange("(k p) -> k p", p=P)),
                (vrows[48:56, :], attn_pre_gain.rearrange("(k p) -> k p", p=P)),
                (vrows[56:64, :], attn_post_gain.rearrange("(k p) -> k p", p=P)),
                (vrows[64:72, :], mlp_pre_gain.rearrange("(k p) -> k p", p=P)),
                (vrows[72:80, :], mlp_post_gain.rearrange("(k p) -> k p", p=P)),
                (vrows[80:82, :], b_gk.rearrange("(k p) -> k p", p=P)),
            ]
            for dst, src in vectors:
                sp.dma_start(dst, src).then_inc(S["small_in"], 16)

            def load_chunk(s):
                kind, n = chunks[s]
                if s >= 3:
                    wait_used(sp, s - 3)
                src = w_ada[:, n * 512:(n + 1) * 512] if kind == "ada" else w_in[:, n:n + 512]
                sp.dma_start(chunk_buf(s), src.rearrange("(k p) n -> p k n", p=P)).then_inc(stream[s % 3], 16)

            load_chunk(0)
            sp.dma_start(x_sb, x.rearrange("b (i p) n -> p (b i) n", p=P)).then_inc(S["x_in"], 16)
            load_chunk(1)
            load_chunk(2)
            load_chunk(3)
            sp.dma_start(bias_raw[:, 0:2 * D], b_e_in).then_inc(S["bias_in"], 16)
            sp.dma_start(bias_raw[:, 2 * D:3 * D], b_e_out).then_inc(S["bias_in"], 16)
            w_in_k = w_in.rearrange("(k p) n -> p k n", p=P)
            sp.wait_ge(S["consts"], 1)
            sp.dma_start(wzf[:, :, 0:LR], w_in_k[:, :, C_Z:C_Z + LR]).then_inc(S["fx_in"], 16)
            sp.dma_start(wzf[:, :, 32:40], w_in_k[:, :, C_FF:C_FF + FH]).then_inc(S["fx_in"], 16)
            sp.dma_start(bf_col[32:40, :], b_f.rearrange("(h a) -> h a", a=1)).then_inc(S["fx_in"], 16)
            sp.dma_start(wgk[:, :], w_gk2).then_inc(S["fx_in"], 16)
            sp.dma_start(gain_bc[:, :], gla_norm_gain.rearrange("(a n) -> a n", a=1).to_broadcast([P, T])).then_inc(S["fx_in"], 16)
            sp.dma_start(br_bc[:, :], b_router.rearrange("(a n) -> a n", a=1).to_broadcast([P, E])).then_inc(S["fx_in"], 16)
            sp.dma_start(w_r[:, :, :], w_router.rearrange("(k p) n -> p k n", p=P)).then_inc(S["fx_in"], 16)
            for s in range(4, len(chunks)):
                load_chunk(s)
                if s == 6:
                    sp.wait_ge(S["bias_split"], 1)
                    sp.dma_start(bias_dram, bias3).then_inc(S["bias_out"], 16)
                    sp.wait_ge(S["fx_cum"], 2)
                    sp.wait_ge(S["consts"], 2)
                    sp.dma_start(qa[65:66, :, :], fwork[32:40, 2, :]).then_inc(S["fx_in"], 16)
                    sp.dma_start(ka[64:65, :, :], fwork[32:40, 3, :]).then_inc(S["fx_in"], 16)
                    zeros = region_m[:, 7168:8192]
                    for b in range(2):
                        for i in range(TT):
                            sp.dma_start(acc_rows(i, b), zeros).then_inc(S["acc_zero"], 16)
                        sp.dma_start(acc_dram[b][0:P, :], zeros[:, 0:512]).then_inc(S["acc_zero"], 16)
            wait_used(sp, len(chunks) - 2)
            sp.dma_start(wo_sb, w_o.rearrange("(k p) n -> p k n", p=P)).then_inc(S["wo_in"], 16)

            def load_up(e, j):
                sp.dma_start(slot(j), w_e_in[e, j * P:(j + 1) * P, :]).then_inc(w_slot[j], 16)

            def load_down(e, j):
                src = w_e_out[e, j * 2 * P:(j + 1) * 2 * P, :].rearrange("(k p) n -> p k n", p=P)
                sp.dma_start(slot(8 + j).rearrange("p (k n) -> p k n", k=2), src).then_inc(w_slot[8 + j], 16)

            sp.wait_ge(S["vec_ready"], 1)
            sp.dma_start(vec_dram.rearrange("a (k p) -> (a k) p", p=P), mrow[0:32, 0, :]).then_inc(S["vec_out"], 16)
            sp.wait_ge(S["vec_out"], 16)
            for n, dst in enumerate((pga, gm, sm)):
                sp.dma_start(dst[:, :], vec_dram[n:n + 1, :].to_broadcast([P, D])).then_inc(S["bc_in"], 16)

            wait_used(sp, len(chunks) - 1)
            load_up(0, 4)
            load_up(0, 5)
            sp.wait_ge(S["pv_done"], len(units))
            sp.wait_ge(S["bias_out"], 16)
            sp.dma_start(bup, bias_dram[0, :, 0:2 * D]).then_inc(S["up_bias_in"], 16)
            sp.dma_start(bdn, bias_dram[0, :, 2 * D:3 * D]).then_inc(S["dn_bias_in"], 16)
            sp.dma_start(x1, x.rearrange("b (i p) n -> p (b i) n", p=P)).then_inc(S["x1_in"], 16)
            for j in (6, 7):
                load_up(0, j)
            for j in range(4):
                load_down(0, j)
            sp.wait_ge(S["wo_mm"], TT)
            for j in range(4):
                load_up(0, j)

            sp.wait_ge(S["h2_done"], TT)
            sp.dma_start(gm[:, :], vec_dram[3:4, :].to_broadcast([P, D])).then_inc(S["bc_in"], 16)

            def up_weights(e, done):
                for j in range(8):
                    sp.wait_ge(S["win_used"], done * 8 + (j + 1))
                    load_up(e, j)

            def up_bias(e, done):
                sp.wait_ge(S["up_bias_used"], done + 1)
                sp.dma_start(bup, bias_dram[e, :, 0:2 * D]).then_inc(S["up_bias_in"], 16)

            def down_weights(e, done):
                sp.wait_ge(S["dn_bias_used"], done + 1)
                sp.dma_start(bdn, bias_dram[e, :, 2 * D:3 * D]).then_inc(S["dn_bias_in"], 16)
                for j in range(4):
                    sp.wait_ge(S["wout_used"], done * 4 + (j + 1))
                    load_down(e, j)

            def last_visit(q):
                return sp.value_load(visits[0:1, 3, bass.ds(q, 1)], min_val=0, max_val=NV - 1)

            def expert(q):
                return sp.value_load(visits[0:1, 2, bass.ds(q, 1)], min_val=0, max_val=E - 1)

            sp.wait_ge(S["visits_ready"], 1)
            e, done = expert(1), last_visit(0)
            up_bias(e, done)
            up_weights(e, done)
            with sp.Fori(2, E) as q:
                e, done = expert(q), last_visit(q - 1)
                before, done_before = expert(q - 1), last_visit(q - 2)
                with sp.If(done - done_before > 1):
                    down_weights(before, done_before)
                    up_bias(e, done)
                    up_weights(e, done)
                with sp.Else():
                    up_bias(e, done)
                    up_weights(e, done)
                    down_weights(before, done_before)
            down_weights(expert(E - 1), last_visit(E - 2))

            done = last_visit(E - 1)
            for b in range(2):
                sp.wait_ge(scattered[b], done * 16 + 16)
            for i in range(TT):
                sp.dma_start(fin_y(i), acc_rows(i, 0)).then_inc(fin_in[i], 16)
                sp.dma_start(fin_z(i), acc_rows(i, 1)).then_inc(fin_in[i], 16)

        @block.gpsimd
        def _(pool):
            g = nc.gpsimd
            step = [0]

            def link(ins):
                step[0] += 1
                ins.then_inc(S["pool_step"], 1)
                pool.wait_ge(S["pool_step"], step[0])

            link(g.memset(wzf[:, :, :], 0.0))
            link(g.memset(cs_pad[:, :, :], 0.0))
            link(g.memset(ident[:, :], 0.0))
            link(g.affine_select(out=ident[:, :], in_=ident[:, :], compare_op=ALU.not_equal, fill=1.0, base=0,
                                 pattern=[[-1, P]], channel_multiplier=1))
            link(g.memset(half_pow[:, :], -0.5))
            link(g.iota(tid[:, :], pattern=[[P, TT]], base=0, channel_multiplier=1, allow_small_or_imprecise_dtypes=True))
            g.memset(ones[:, :], 1.0).then_inc(S["consts"], 1)

            def power(dst, src, n):
                return g.tensor_tensor(out=dst, in0=src, in1=half_pow[:, 0:n], op=ALU.pow)

            def rms(dst, tmp, src):
                link(g.tensor_scalar(stat[:, tmp:tmp + 1], stat[:, src:src + 1], 1.0 / D, EPS, ALU.mult, ALU.add))
                return power(stat[:, dst:dst + 1], stat[:, tmp:tmp + 1], 1)

            for i in range(TT):
                pool.wait_ge(S["x_sq"], i + 1)
                rms(i, 4 + i, i).then_inc(S["x_rstd"], 1)
            link(g.memset(maskb[:, :], 0.0))
            link(g.affine_select(out=maskb[:, :], in_=maskb[:, :], compare_op=ALU.is_ge, fill=NEG, base=0,
                                 pattern=[[-1, P]], channel_multiplier=1))
            link(g.tensor_copy(identb[:, :], ident[:, :]))
            link(g.memset(before[:, :], 1.0))
            link(g.affine_select(out=before[:, :], in_=before[:, :], compare_op=ALU.is_ge, fill=0.0, base=-1,
                                 pattern=[[1, P]], channel_multiplier=-1))
            link(g.iota(iota[:, :], pattern=[[1, P]], base=0, channel_multiplier=0, allow_small_or_imprecise_dtypes=True))
            link(g.memset(scan_reset[:, :], 1.0))
            link(g.memset(scan_reset[:, :].rearrange("p (n c) -> p n c", c=CH)[:, :, 0:1], 0.0))
            link(g.memset(route_reset[:, :], 1.0))
            link(g.memset(route_reset[:, :].rearrange("p (n c) -> p n c", c=E)[:, :, 0:1], 0.0))
            link(g.memset(ones3[:, :], 1.0))
            pool.wait_ge(S["bias_out"], 16)
            link(g.memset(qa[64:66, :, :], 1.0))
            link(g.memset(ka[64:66, :, :], 1.0))
            link(g.memset(kdz[:, :, :, :], 0.0))
            link(g.memset(qtp[:, :, :], 0.0))
            g.memset(stat[:, 62:63], 0.0).then_inc(S["consts"], 1)
            pool.wait_ge(S["fx_in"], 16 * 7)
            for i in range(TT):
                pool.wait_ge(*taken(out_at[("gg", i)]))
                g.tensor_tensor(out=gs[:, i, :], in0=gs[:, i, :], in1=gain_bc[:, :], op=ALU.mult).then_inc(S["gs_ready"], 1)
            pool.wait_ge(S["bias_split"], 1)
            link(g.memset(attz[:, :, :, :], 0.0))
            pool.wait_ge(S["fx_in"], 16 * 9)
            link(g.memset(state[:, :, :, :], 0.0))
            g.memset(stat[:, 63:64], 0.0).then_inc(S["consts"], 1)
            for i in range(TT):
                pool.wait_ge(S["att_cp"], i + 1)
                g.affine_select(out=attz[:, i % 2, :, :], in_=attz[:, i % 2, :, :], compare_op=ALU.is_ge, fill=0.0,
                                base=0, pattern=[[0, GH], [1, P]], channel_multiplier=-1).then_inc(S["att_ready"], 1)
                if i >= 1:
                    pool.wait_ge(S["go_ms"], i)
                    power(stat[:, 8 + 4 * (i - 1):12 + 4 * (i - 1)], stat[:, 24 + 4 * (i - 1):28 + 4 * (i - 1)], 4).then_inc(S["go_rstd"], 1)
            pool.wait_ge(S["go_ms"], TT)
            power(stat[:, 20:24], stat[:, 36:40], 4).then_inc(S["go_rstd"], 1)
            for i in range(TT):
                pool.wait_ge(S["wo_sq"], i + 1)
                rms(40 + i, 44 + i, 40 + i).then_inc(S["wo_rstd"], 1)
                pool.wait_ge(S["x1_sq"], i + 1)
                rms(48 + i, 52 + i, 48 + i).then_inc(S["x1_rstd"], 1)

            def carry(n=0):
                return g.tensor_tensor(mark[:, n:n + 1], half_pow[:, 0:1], half_pow[:, 1:2], ALU.mult)

            def gather(v, parity, nb):
                now = tok_now[:, parity:parity + 1]
                g.tensor_copy(now, tok[:, bass.ds(v, 1)]).then_inc(S["tok_copied"], 1)
                pool.wait_ge(S["tok_copied"], v + 1)
                carry()
                g.indirect_dma_start(out=xg[parity][0:BLK * nb, :], out_offset=None, in_=h_dram,
                                     in_offset=bass.IndirectOffsetOnAxis(ap=now[0:BLK * nb, :], axis=0)).then_inc(gathered[parity], 16)

            def scatter(v, parity, nb, first=False):
                if not first:
                    for b in range(2):
                        pool.wait_ge(scattered[b], 16 * v)
                    carry(1)
                g.tensor_copy(row_now[:, :], row_col[:, bass.ds(v * 2, 2)]).then_inc(S["row_copied"], 1)
                pool.wait_ge(S["row_copied"], v + 1)
                pool.wait_ge(S["y_evac"], v + 1)
                carry()
                for b in range(nb):
                    g.indirect_dma_start(out=acc_dram[b], out_offset=bass.IndirectOffsetOnAxis(ap=row_now[:, b:b + 1], axis=0),
                                         in_=y_sb[parity][:, b, :], in_offset=None, compute_op=ALU.add).then_inc(scattered[b], 16)
                if nb == 1:
                    g.dma_start(word[:, :], h_dram[0:1, 0:1]).then_inc(scattered[1], 16)

            def by_blocks(v, f):
                n = pool.value_load(visits[0:1, 0, bass.ds(v, 1)], min_val=0, max_val=2)
                with pool.If(n > 1):
                    f(2)
                with pool.Else():
                    f(1)

            pool.wait_ge(S["tok_ready"], 1)
            for b in range(2):
                pool.wait_ge(h2_store[b], 16 * TT // 2)
            gather(0, 0, 2)
            pool.wait_ge(S["lg_mm"], TT)
            gather(1, 1, 2)
            pool.wait_ge(S["visits_ready"], 1)
            for v in (0, 1):
                pool.wait_ge(S["xtr_done"], 2 * v + 2)
                by_blocks(v + 2, lambda nb: gather(v + 2, v % 2, nb))
            pool.wait_ge(S["acc_zero"], 32 * (TT + 1))
            pool.wait_ge(S["col_ready"], 1)
            by_blocks(0, lambda nb: scatter(0, 0, nb, True))
            with pool.Fori(1, E // 2) as pair:
                for parity in range(2):
                    v = pair * 2 + parity
                    pool.wait_ge(S["xtr_done"], 2 * v + 2)
                    by_blocks(v + 2, lambda nb: gather(v + 2, parity, nb))
                    by_blocks(v - 1, lambda nb: scatter(v - 1, 1 - parity, nb))
            by_blocks(E - 1, lambda nb: scatter(E - 1, 1, nb))

            def extra(v, parity, then=None):
                n = pool.value_load(visits[0:1, 0, bass.ds(v, 1)], min_val=0, max_val=2)
                with pool.If(n > 0):
                    pool.wait_ge(S["xtr_done"], 2 * v + 2)
                    by_blocks(v + 2, lambda nb: gather(v + 2, parity, nb))
                    by_blocks(v, lambda nb: scatter(v, parity, nb))
                    if then:
                        then()

            with pool.Fori(0, GROUPS) as group:
                some = pool.value_load(visits[0:1, 0, bass.ds(group * (2 * PAIRS) + E, 1)], min_val=0, max_val=2)
                with pool.If(some > 0):
                    with pool.Fori(0, PAIRS) as pair:
                        v = group * (2 * PAIRS) + pair * 2 + E
                        extra(v, 0, lambda: extra(v + 1, 1))

            for i in range(TT):
                pool.wait_ge(S["fin_sq"], i + 1)
                rms(56 + i, 4 + i, 56 + i).then_inc(S["fin_rstd"], 1)

        @block.scalar
        def _(act):
            a_ = nc.scalar
            step = [0]

            def link(ins):
                step[0] += 1
                ins.then_inc(S["act_step"], 1)
                act.wait_ge(S["act_step"], step[0])

            act.wait_ge(S["crow_in"], 16)
            a_.activation(fwork[0:KT, 0, 0:P], crow[:, :], ACT.Sigmoid).then_inc(S["cs_ready"], 1)
            act.wait_ge(S["x_in"], 16)
            for i in range(TT):
                a_.activation(region_h[:, i * D:(i + 1) * D], x_sb[:, i, :], ACT.Square, accum_out=stat[:, i:i + 1]).then_inc(S["x_sq"], 1)

            act.wait_ge(S["ga_ready"], 1)
            for k in range(1, KT, 2):
                act.wait_ge(S["xt_mm"], k + 1)
                a_.activation(hT[:, k, :], bank[:, 4 + k % 4, :], ACT.Identity, scale=ga[:, k:k + 1],
                              bias=modT[:, k:k + 1]).then_inc(S["ht_act"], 1)

            gg_done = 0
            for j, (kind, a, who) in enumerate(outs):
                src = bank[:, j % 4, :]
                if kind == "gk":
                    act.wait_ge(S["proj_mm"], j + 1)
                    a_.activation(etmp[:, a, :], src, ACT.Abs, bias=vcol[:, 80 + a:81 + a]).then_inc(S["gk_abs"], 1)
                    if a == 1:
                        act.wait_ge(S["gk_abs"], 2)
                        link(a_.activation(etmp[:, :, :], etmp[:, :, :], ACT.Exp, scale=-1.0))
                        a_.activation(etmp[:, :, :], etmp[:, :, :], ACT.Ln, bias=1.0).then_inc(S["gk_ln"], 1)
                        act.wait_ge(S["cum_done"], 2)
                        link(a_.activation(etmp[:, :, :], cumT[:, :, :], ACT.Exp, scale=1.0 / GLA_NORM))
                        a_.activation(dec[:, :, :], cumT.rearrange("p a (n c) -> p a n c", c=CH)[:, :, :, CH - 1],
                                      ACT.Exp, scale=1.0 / GLA_NORM).then_inc(S["dec_done"], 1)
                        act.wait_ge(S["dec_done"], 1)
                        a_.activation(gtmp[:, :, :], cumT[:, :, :], ACT.Exp, scale=-1.0 / GLA_NORM).then_inc(S["enb_done"], 1)
                        act.wait_ge(S["dd_done"], 2)
                        a_.activation(etmp[:, :, :], etmp[:, :, :], ACT.Exp, scale=1.0 / GLA_NORM).then_inc(S["dk_done"], 1)
                    continue
                if kind == "gg":
                    act.wait_ge(S["proj_mm"], j + 1)
                    if a >= 2:
                        act.wait_ge(*taken(out_at[("gg", a - 2)]))
                    a_.activation(prob[:, a % 2, :], src, ACT.Sigmoid).then_inc(S["sig_done"], 1)
                    continue
                if who != "act":
                    continue
                act.wait_ge(S["proj_mm"], j + 1)
                if kind == "zf":
                    a_.activation(zf[:, :], bank[0:40, j % 4, :], ACT.Copy).then_inc(S["ev_act"], 1)
                    act.wait_ge(S["ev_act"], 1)
                    act.wait_ge(S["fx_in"], 16 * 7)
                    act.wait_ge(S["csT_ev"], 1)
                    link(a_.activation(fwork[32:40, 0, :], zf[32:40, :], ACT.Abs, bias=bf_col[32:40, :]))
                    link(a_.activation(fwork[32:40, 0, :], fwork[32:40, 0, :], ACT.Exp, scale=-1.0))
                    a_.activation(fwork[32:40, 0, :], fwork[32:40, 0, :], ACT.Ln, bias=1.0).then_inc(S["fx_ln"], 1)
                elif kind in ("qg", "kg"):
                    if kind == "qg" and a == 0:
                        act.wait_ge(S["xt_mm"], KT)
                    dst = (qg_raw if kind == "qg" else kg_raw)[:, a, :]
                    a_.activation(dst, src, ACT.Copy).then_inc(S["ev_act"], 1)
                elif kind == "vg":
                    a_.activation(vg[:, a, :], src, ACT.Copy).then_inc(S["ev_act"], 1)
                elif kind == "vf":
                    a_.activation(vf[:, a, :], src, ACT.Copy).then_inc(S["ev_act"], 1)
                else:
                    dst, scale = (ka, 1.0) if kind == "kf" else (qa, FD ** -0.5)
                    act.wait_ge(S["consts"], 2)
                    a_.activation(dst[0:64, 2 * a, :], src[0:64, :], ACT.Copy, scale=scale)
                    a_.activation(dst[0:64, 2 * a + 1, :], src[64:128, :], ACT.Copy, scale=scale).then_inc(S["ev_act"], 1)

            def gla_scores(i):
                act.wait_ge(S["att_mm"], i + 1)
                act.wait_ge(S["consts"], 3)
                if i >= 2:
                    act.wait_ge(S["go_mm"], i - 1)
                src = bank[:, i % 2, :].rearrange("p (h n) -> p h n", h=GH)
                a_.activation(attz[0:64, i % 2, :, 0:64], src[0:64, :, 0:64], ACT.Copy)
                a_.activation(attz[64:128, i % 2, :, 64:128], src[64:128, :, 64:128], ACT.Copy).then_inc(S["att_cp"], 1)

            def gla_out(i):
                act.wait_ge(S["go_mm"], i + 1)
                if i >= 1:
                    act.wait_ge(S["mixg"], i)
                a_.activation(osb[:, :], bank[:, 5 + i % 2, :], ACT.Copy).then_inc(S["go_ev"], 1)

            gla_scores(0)
            for i in range(1, TT):
                gla_scores(i)
                gla_out(i - 1)

            def fox_exp(u):
                qi, h = units[u]
                act.wait_ge(S["max_done"], u + 1)
                if u >= 3:
                    act.wait_ge(S["pt_done"], u - 2)
                n = (qi + 1) * P
                a_.activation(probs[u % 3][:, 0:n], bank[:, u % 3, 0:n], ACT.Exp, bias=nmax[:, u % 4:u % 4 + 1],
                              accum_out=rsum[:, u:u + 1]).then_inc(S["exp_done"], 1)

            def fox_take(u):
                qi, h = units[u]
                act.wait_ge(S["pt_done"], u + 1)
                if u >= 2:
                    act.wait_ge(S["pv_done"], u - 1)
                n = (qi + 1) * P
                a_.activation(probT[:, u % 2, 0:n], bank[:, 3 + u % 2, 0:n], ACT.Copy).then_inc(S["pt_ev"], 1)

            fox_exp(0)
            gla_out(TT - 1)
            for u in range(1, len(units) + 2):
                if u < len(units):
                    fox_exp(u)
                if u >= 2:
                    fox_take(u - 2)

            for i in range(TT):
                act.wait_ge(S["wo_mm"], i + 1)
                if i >= 1:
                    act.wait_ge(S["x1_sq"], i)
                a_.activation(ytmp[:, :], bank[:, 2 * (i % 2):2 * (i % 2) + 2, :], ACT.Square,
                              accum_out=stat[:, 40 + i:41 + i]).then_inc(S["wo_sq"], 1)
                act.wait_ge(S["x1_done"], i + 1)
                a_.activation(ytmp[:, :], x1[:, i, :], ACT.Square, accum_out=stat[:, 48 + i:49 + i]).then_inc(S["x1_sq"], 1)
                act.wait_ge(S["h2_done"], i + 1)
                act.dma_start(h_dram[i * P:(i + 1) * P, :], h2[:, i % 2, :]).then_inc(h2_store[i % 2], 16)
                act.wait_ge(S["h2t_mm"], i + 1)
                if i >= 2:
                    act.wait_ge(S["lg_mm"], i - 1)
                a_.activation(h2T[:, i % 2, :, :], bank[:, 4:6, :], ACT.Copy).then_inc(S["h2t_ev"], 1)
            act.wait_ge(S["r_sub"], 1)
            a_.activation(rw("ex"), rw("sub"), ACT.Exp).then_inc(S["r_exp"], 1)

            def take_xT(v, nb):
                for half in range(2):
                    act.wait_ge(S["xtr_done"], 2 * v + half + 1)
                    a_.activation(xT[:, 4 * half:4 * half + 4, 0:BLK * nb],
                                  bank[:, 4 + half, :].rearrange("p (k s) -> p k s", k=4)[:, :, 0:BLK * nb], ACT.Copy).then_inc(S["xt_ready"], 1)

            def take_aT(v, nb):
                act.wait_ge(S["atr_done"], v + 1)
                a_.activation(aT[:, 0:nb, :, :], bank[:, 4:4 + nb, :], ACT.Copy).then_inc(S["at_ready"], 1)

            def sigmoid(v, nb):
                act.wait_ge(S["g_ready"], v + 1)
                a_.activation(s_sb[:, 0:nb, :], g_sb[:, 0:nb, :], ACT.Sigmoid, scale=ALPHA).then_inc(S["s_ready"], 1)

            def gate_y(v, parity, nb, first=False):
                act.wait_ge(S["wout_used"], 4 * (v + 1))
                if not first:
                    for b in range(2):
                        act.wait_ge(scattered[b], 16 * v - 16)
                a_.activation(mark[:, 3:4], half_pow[:, 0:1], ACT.Copy)
                for b in range(nb):
                    ins = a_.activation(y_sb[parity][:, b, :], bank[:, 6 + b, :], ACT.Copy, scale=gate_col[:, bass.ds(v * 2 + b, 1)])
                ins.then_inc(S["y_evac"], 1)

            def by_blocks(v, *steps):
                n = act.value_load(visits[0:1, 0, bass.ds(v, 1)], min_val=0, max_val=2)
                with act.If(n > 1):
                    for f in steps:
                        f(2)
                with act.Else():
                    for f in steps:
                        f(1)

            take_xT(0, 2)
            act.wait_ge(S["visits_ready"], 1)
            by_blocks(1, lambda nb: take_xT(1, nb))
            by_blocks(0, lambda nb: sigmoid(0, nb), lambda nb: take_aT(0, nb))
            by_blocks(2, lambda nb: take_xT(2, nb))
            by_blocks(1, lambda nb: sigmoid(1, nb))
            act.wait_ge(S["col_ready"], 1)
            by_blocks(0, lambda nb: gate_y(0, 0, nb, True))
            def visit(v, parity, first=False):
                by_blocks(v - 1, lambda nb: take_aT(v - 1, nb))
                by_blocks(v + 1, lambda nb: take_xT(v + 1, nb))
                by_blocks(v, lambda nb: sigmoid(v, nb))
                by_blocks(v - 1, lambda nb: gate_y(v - 1, 1 - parity, nb, first))

            visit(2, 0, True)
            visit(3, 1)
            with act.Fori(2, E // 2) as pair:
                for parity in range(2):
                    visit(pair * 2 + parity, parity)
            by_blocks(E - 1, lambda nb: take_aT(E - 1, nb), lambda nb: gate_y(E - 1, 1, nb))

            def extra(v, parity, then=None):
                n = act.value_load(visits[0:1, 0, bass.ds(v, 1)], min_val=0, max_val=2)
                with act.If(n > 0):
                    by_blocks(v + 1, lambda nb: take_xT(v + 1, nb))
                    by_blocks(v, lambda nb: sigmoid(v, nb), lambda nb: take_aT(v, nb), lambda nb: gate_y(v, parity, nb))
                    if then:
                        then()

            with act.Fori(0, GROUPS) as group:
                some = act.value_load(visits[0:1, 0, bass.ds(group * (2 * PAIRS) + E, 1)], min_val=0, max_val=2)
                with act.If(some > 0):
                    with act.Fori(0, PAIRS) as pair:
                        v = group * (2 * PAIRS) + pair * 2 + E
                        extra(v, 0, lambda: extra(v + 1, 1))

            for i in range(TT):
                act.wait_ge(S["yacc"], i + 1)
                a_.activation(region_m[:, i * D:(i + 1) * D], fin_y(i), ACT.Square, accum_out=stat[:, 56 + i:57 + i]).then_inc(S["fin_sq"], 1)
            for i in range(TT):
                act.wait_ge(S["fin_done"], i + 1)
                act.dma_start(out[0, i * P:(i + 1) * P, :], x1[:, i, :]).then_inc(S["out_done"], 16)
            act.wait_ge(S["out_done"], 16 * TT)

        @block.vector
        def _(dve):
            v_ = nc.vector
            step = [0]

            def link(ins):
                step[0] += 1
                ins.then_inc(S["dve_step"], 1)
                dve.wait_ge(S["dve_step"], step[0])

            dve.wait_ge(S["cs_ready"], 1)
            v_.tensor_tensor(crow[:, :], crow[:, :], fwork[0:KT, 0, 0:P], ALU.mult).then_inc(S["csT_done"], 1)
            dve.wait_ge(S["consts"], 1)
            dve.wait_ge(S["vr_done"], 2)
            v_.tensor_copy(vcol[:, :], bank[:, 3, 0:82]).then_inc(S["vcol_ready"], 1)
            v_.tensor_copy(cs_pad[:, :, 0], bank[:, 2, 0:KT]).then_inc(S["csT_ev"], 1)

            def ada_row(n):
                dve.wait_ge(S["ada_mm"], n + 1)
                v_.tensor_copy(mrow[:, n % 2, :], bank[:, ada_bank(n), 0:P]).then_inc(S["ada_row"], 1)

            def ada_col(n):
                dve.wait_ge(S["ada_tr"], n + 1)
                v_.tensor_tensor(modT[:, 4 * n:4 * n + 4], bank[:, ada_bank(n) + 2, 0:P:32], vcol[:, 4 * n:4 * n + 4],
                                 ALU.add).then_inc(S["ada_col"], 1)

            dve.wait_ge(S["vcol_ready"], 1)
            ada_row(0)
            ada_col(0)
            for i in range(TT):
                dve.wait_ge(S["x_rstd"], i + 1)
                v_.tensor_scalar(x_sb[:, i, :], x_sb[:, i, :], stat[:, i:i + 1], None, ALU.mult).then_inc(S["x_norm"], 1)
            for n in range(1, 4):
                ada_row(n)
                ada_col(n)
            dve.wait_ge(S["ada_col"], 4)
            v_.scalar_tensor_tensor(ga[:, :], modT[:, 8:16], 1.0, vcol[:, 48:56], ALU.add, ALU.mult).then_inc(S["ga_ready"], 1)
            dve.wait_ge(S["ga_ready"], 1)
            for k in range(0, KT, 2):
                dve.wait_ge(S["xt_mm"], k + 1)
                v_.tensor_scalar(hT[:, k, :], bank[:, 4 + k % 4, :], ga[:, k:k + 1], modT[:, k:k + 1],
                                 ALU.mult, ALU.add).then_inc(S["ht_dve"], 1)

            def gla_operands():
                dve.wait_ge(S["gk_ln"], 1)
                dve.wait_ge(S["consts"], 2)
                for a in range(2):
                    link(v_.tensor_tensor(gtmp[:, a, :], cumT[:, a, :], etmp[:, a, :], ALU.subtract))
                    v_.tensor_tensor_scan(cumT[:, a, :], scan_reset[:, :], gtmp[:, a, :], 0.0, ALU.mult, ALU.add).then_inc(S["cum_done"], 1)
                dve.wait_ge(S["dec_done"], 1)
                wait_out(dve, "qg")
                wait_out(dve, "kg")
                for h in range(GH):
                    r = slice(64 * (h % 2), 64 * (h % 2) + 64)
                    ins = v_.scalar_tensor_tensor(qtp[r, h, :], qg_raw[r, h // 2, :], GK ** -0.5, etmp[r, h // 2, :],
                                                  ALU.mult, ALU.mult)
                link(ins)
                cum = cumT.rearrange("p a (n c) -> p a n c", c=CH)
                for a in range(2):
                    v_.tensor_tensor(etmp[:, a, :].rearrange("p (n c) -> p n c", c=CH),
                                     cum[:, a, :, CH - 1:CH].to_broadcast([P, T // CH, CH]), cum[:, a, :, :],
                                     ALU.subtract).then_inc(S["dd_done"], 1)
                dve.wait_ge(S["enb_done"], 1)
                v_.tensor_tensor(ktT[:, :, :], kg_raw[:, :, :], gtmp[:, :, :], ALU.mult).then_inc(S["gla_ready"], 1)
                dve.wait_ge(S["dk_done"], 1)
                v_.tensor_tensor(kdT[:, :, :], kg_raw[:, :, :], etmp[:, :, :], ALU.mult).then_inc(S["gla_ready"], 1)

            def take_output(j, kind, a, who):
                src = bank[:, j % 4, :]
                if kind == "zf":
                    dve.wait_ge(S["ev_act"], 1)
                    dve.wait_ge(S["fx_in"], 16 * 7)
                    link(v_.tensor_scalar(fwork[32:40, 1, :], zf[32:40, :], bf_col[32:40, :], 0.0, ALU.add, ALU.min))
                    dve.wait_ge(S["fx_ln"], 1)
                    link(v_.tensor_tensor(fwork[32:40, 1, :], fwork[32:40, 1, :], fwork[32:40, 0, :], ALU.subtract))
                    link(v_.memset(fwork[32:40, 0, :], 0.0))
                    v_.tensor_tensor_scan(fwork[32:40, 2, :], fwork[32:40, 1, :], fwork[32:40, 0, :], 0.0, ALU.add, ALU.add).then_inc(S["fx_cum"], 1)
                    dve.wait_ge(S["fx_cum"], 1)
                    v_.tensor_scalar(fwork[32:40, 3, :], fwork[32:40, 2, :], -1.0, None, ALU.mult).then_inc(S["fx_cum"], 1)
                    dve.wait_ge(S["bias_in"], 32)
                    for part in range(2):
                        link(v_.tensor_copy(bias3[:, part, :], bias_raw))
                        link(v_.tensor_tensor(bias_raw, bias_raw, bias3[:, part, :], ALU.subtract))
                    v_.tensor_copy(bias3[:, 2, :], bias_raw).then_inc(S["bias_split"], 1)
                if who != "dve":
                    return
                if kind == "gk":
                    dve.wait_ge(S["gk_abs"], a + 1)
                    dve.wait_ge(S["xt_mm"], KT)
                    v_.tensor_scalar(cumT[:, a, :], src, vcol[:, 80 + a:81 + a], 0.0, ALU.add, ALU.min).then_inc(S["ev_dve"], 1)
                    if a == 1:
                        dve.wait_ge(S["ev_dve"], taken(j)[1])
                        gla_operands()
                elif kind == "gg":
                    dve.wait_ge(S["sig_done"], a + 1)
                    v_.tensor_tensor(gs[:, a, :], src, prob[:, a % 2, :], ALU.mult).then_inc(S["ev_dve"], 1)
                else:
                    dve.wait_ge(S["proj_mm"], j + 1)
                    if kind == "vf":
                        v_.tensor_copy(vf[:, a, :], src).then_inc(S["ev_dve"], 1)
                    else:
                        dst, scale = (ka, 1.0) if kind == "kf" else (qa, FD ** -0.5)
                        dve.wait_ge(S["consts"], 2)
                        v_.tensor_scalar(dst[0:64, 2 * a, :], src[0:64, :], scale, None, ALU.mult)
                        v_.tensor_scalar(dst[0:64, 2 * a + 1, :], src[64:128, :], scale, None, ALU.mult).then_inc(S["ev_dve"], 1)

            for j, (kind, a, who) in enumerate(outs):
                take_output(j, kind, a, who)
                for n in range(4, 12):
                    if ada_behind[n] == j:
                        ada_row(n)
                for n in range(4, 12):
                    if ada_turned[n] == j:
                        ada_col(n)

            dve.wait_ge(S["ada_col"], 12)
            v_.tensor_tensor(cols[:, 0, :], modT[:, 16:24], vcol[:, 56:64], ALU.mult)
            v_.scalar_tensor_tensor(cols[:, 1, :], modT[:, 32:40], 1.0, vcol[:, 64:72], ALU.add, ALU.mult)
            v_.tensor_copy(cols[:, 2, :], modT[:, 24:32])
            v_.tensor_tensor(cols[:, 3, :], modT[:, 40:48], vcol[:, 72:80], ALU.mult).then_inc(S["cols_ready"], 1)
            dve.wait_ge(S["cols_ready"], 1)
            dve.wait_ge(S["colT_mm"], 1)
            v_.tensor_copy(mrow[0:32, 0, :], bank[0:32, 7, 0:P]).then_inc(S["vec_ready"], 1)

            def kd_take(i):
                dve.wait_ge(S["kd_mm"], i + 1)
                if i == 0:
                    dve.wait_ge(S["acc_zero"], 32 * (TT + 1))
                if i >= 2:
                    dve.wait_ge(S["kv_mm"], 2 * (i - 1))
                for ch in range(2):
                    r = slice(64 * ch, 64 * ch + 64)
                    ins = v_.tensor_copy(kdz[r, i % 2, ch, :], bank[r, 2, 0:256])
                ins.then_inc(S["kd_ev"], 1)

            def st_update(n):
                dve.wait_ge(S["kv_mm"], n + 1)
                if n >= 3:
                    dve.wait_ge(S["go_mm"], (n - 3) // 2 + 1)
                if n:
                    dve.wait_ge(S["st_done"], n)
                else:
                    dve.wait_ge(S["consts"], 3)
                for h in range(GH):
                    r = slice(64 * (h % 2), 64 * (h % 2) + 64)
                    ins = v_.scalar_tensor_tensor(state[r, (n + 1) % 4, h, :], state[r, n % 4, h, :],
                                                  dec[r, h // 2, n:n + 1], bank[r, 3 + n % 2, h * P:(h + 1) * P],
                                                  ALU.mult, ALU.add)
                ins.then_inc(S["st_done"], 1)

            def gla_post(i):
                dve.wait_ge(S["go_ev"], i + 1)
                link(v_.tensor_tensor(osq[:, :], osb[:, :], osb[:, :], ALU.mult))
                ms = stat[:, 24 + 4 * i:28 + 4 * i]
                link(v_.tensor_reduce(ms, osq.rearrange("p (h n) -> p h n", h=GH), AX.X, ALU.add))
                v_.tensor_scalar(ms, ms, 1.0 / GV, EPS, ALU.mult, ALU.add).then_inc(S["go_ms"], 1)
                dve.wait_ge(S["go_rstd"], i + 1)
                rs = stat[:, 8 + 4 * i:12 + 4 * i].rearrange("p (h a) -> p h a", a=1).to_broadcast([P, GH, GV])
                link(v_.tensor_tensor(osq.rearrange("p (h n) -> p h n", h=GH), osb.rearrange("p (h n) -> p h n", h=GH), rs, ALU.mult))
                dve.wait_ge(S["gs_ready"], i + 1)
                v_.tensor_tensor(mix[:, i, 0:512], osq[:, :], gs[:, i, :], ALU.mult).then_inc(S["mixg"], 1)

            kd_take(0)
            for i in range(TT):
                if i + 1 < TT:
                    kd_take(i + 1)
                for n in (2 * i, 2 * i + 1):
                    if n < 7:
                        st_update(n)
                if i >= 1:
                    gla_post(i - 1)

            def fox_max(u):
                qi, h = units[u]
                dve.wait_ge(S["s_done"], u + 1)
                if u >= 4:
                    dve.wait_ge(S["exp_done"], u - 3)
                v_.tensor_reduce(nmax[:, u % 4:u % 4 + 1], bank[:, u % 3, 0:(qi + 1) * P], AX.X, ALU.max,
                                 negate=True).then_inc(S["max_done"], 1)

            def fox_norm(u):
                qi, h = units[u]
                dve.wait_ge(S["exp_done"], u + 1)
                link(v_.reciprocal(rcp[:, h:h + 1], rsum[:, u:u + 1]))
                row = probs[u % 3][:, 0:(qi + 1) * P]
                v_.tensor_scalar(row, row, rcp[:, h:h + 1], None, ALU.mult).then_inc(S["norm_done"], 1)

            def fox_out(qi):
                dve.wait_ge(S["pv_done"], 8 * qi + 8)
                v_.tensor_copy(mixT[:, 4:8, qi * P:(qi + 1) * P],
                               bank[:, 5 + qi % 2, :].rearrange("p (k t) -> p k t", k=4)).then_inc(S["mixf"], 1)

            def mixT_take(qi):
                dve.wait_ge(S["mt_mm"], qi + 1)
                v_.tensor_copy(mixT[:, 0:4, qi * P:(qi + 1) * P],
                               bank[:, 7, :].rearrange("p (k t) -> p k t", k=4)).then_inc(S["mt_ev"], 1)

            for w in range(8 * TT + 4):
                if w < len(units):
                    fox_max(w)
                if 1 <= w <= len(units):
                    fox_norm(w - 1)
                if w == 1:
                    gla_post(TT - 1)
                for qi in range(TT):
                    if w == 8 * qi + 6:
                        mixT_take(qi)
                    if w == 8 * qi + 11:
                        fox_out(qi)

            def take_logits(i):
                dve.wait_ge(S["lg_mm"], i + 1)
                v_.tensor_tensor(lg[:, i, :], bank[:, 6, i * E:(i + 1) * E], br_bc[:, :], ALU.add).then_inc(S["lg_done"], 1)

            dve.wait_ge(S["x1_in"], 16)
            dve.wait_ge(S["bc_in"], 16 * 3)
            for i in range(TT):
                dve.wait_ge(S["wo_sq"], i + 1)
                link(v_.tensor_tensor(ynorm.rearrange("p (b n) -> p b n", b=2), bank[:, 2 * (i % 2):2 * (i % 2) + 2, :],
                                      pga.rearrange("p (b n) -> p b n", b=2), ALU.mult))
                dve.wait_ge(S["wo_rstd"], i + 1)
                v_.scalar_tensor_tensor(x1[:, i, :], ynorm[:, :], stat[:, 40 + i:41 + i], x1[:, i, :], ALU.mult, ALU.add).then_inc(S["x1_done"], 1)
                if i >= 2:
                    dve.wait_ge(h2_store[i % 2], 16 * (i // 2))
                    dve.wait_ge(S["h2t_mm"], i - 1)
                else:
                    dve.wait_ge(S["mt_mm"], TT)
                dve.wait_ge(S["x1_done"], i + 1)
                link(v_.tensor_tensor(h2[:, i % 2, :], x1[:, i, :], gm[:, :], ALU.mult))
                dve.wait_ge(S["x1_rstd"], i + 1)
                v_.scalar_tensor_tensor(h2[:, i % 2, :], h2[:, i % 2, :], stat[:, 48 + i:49 + i], sm[:, :], ALU.mult, ALU.add).then_inc(S["h2_done"], 1)
                if i >= 1:
                    take_logits(i - 1)
            take_logits(TT - 1)
            dve.wait_ge(S["lg_done"], TT)

            top = small[:, 0:32].rearrange("p (i n) -> p i n", i=TT)
            for i in range(TT):
                ins = v_.max(top[:, i, :], lg[:, i, :])
            link(ins)
            shape = [P, TT, E]
            fourth = top[:, :, 3:4].to_broadcast(shape)
            v_.tensor_tensor(rw("sub"), lg[:, :, :], top[:, :, 0:1].to_broadcast(shape), ALU.subtract).then_inc(S["r_sub"], 1)
            v_.tensor_tensor(rw("gt"), lg[:, :, :], fourth, ALU.is_gt)
            link(v_.tensor_tensor(rw("eq"), lg[:, :, :], fourth, ALU.is_equal))
            left = small[:, 32:36]
            v_.tensor_reduce(left, rw("gt"), AX.X, ALU.add)
            flat = lambda n: rw(n).rearrange("p i e -> p (i e)")
            link(v_.tensor_tensor_scan(flat("eqc"), route_reset[:, :], flat("eq"), 0.0, ALU.mult, ALU.add))
            link(v_.tensor_scalar(left, left, -1.0, float(TOPK), ALU.mult, ALU.add))
            link(v_.tensor_tensor(rw("eqc"), rw("eqc"), left.rearrange("p (i a) -> p i a", a=1).to_broadcast(shape), ALU.is_le))
            link(v_.tensor_tensor(rw("eq"), rw("eq"), rw("eqc"), ALU.mult))
            v_.tensor_tensor(mask_bf.rearrange("p (i e) -> p i e", i=TT), rw("gt"), rw("eq"), ALU.add).then_inc(S["r_mask"], 1)
            link(v_.tensor_tensor(rw("mask"), rw("gt"), rw("eq"), ALU.add))
            link(v_.tensor_tensor_scan(flat("rk"), route_reset[:, :], flat("mask"), 0.0, ALU.mult, ALU.add))
            link(v_.tensor_tensor(rw("rk"), rw("rk"), rw("mask"), ALU.mult))
            for k in range(TOPK):
                v_.tensor_scalar(sel4[:, :, k, :], rw("rk"), float(k + 1), None, ALU.is_equal).then_inc(S["sel_ready"], 1)

            def select(name, dst):
                row = rw(name).rearrange("p i (a e) -> p i a e", a=1).to_broadcast([P, TT, TOPK, E])
                link(v_.tensor_tensor(prod4[:, :, :, :], sel4[:, :, :, :], row, ALU.mult))
                link(v_.tensor_reduce(dst.rearrange("p (i k) -> p i k", i=TT), prod4[:, :, :, :], AX.X, ALU.add))

            cnt, nvis, vend, vstart, ended, own, part = (small[:, 64 + E * n:64 + E * (n + 1)] for n in range(7))
            order, heavy, hs, h_at, l_at, p_light, p_heavy, own_col, own_n, here = (
                region_h[:, 1152 + E * n:1152 + E * (n + 1)] for n in range(10))
            dve.wait_ge(S["pos_mm"], 1)
            link(v_.tensor_copy(cnt, bank[:, 5, 0:E]))
            link(v_.tensor_scalar(nvis, cnt, float(P), 1.0, ALU.is_gt, ALU.add))
            link(v_.scalar_tensor_tensor(nvis, cnt, 2.0 * P, nvis, ALU.is_gt, ALU.add))
            link(v_.scalar_tensor_tensor(nvis, cnt, 3.0 * P, nvis, ALU.is_gt, ALU.add))
            tail = slice(1, E)
            link(v_.tensor_scalar(heavy, cnt, float(BLK), None, ALU.is_gt))
            v_.tensor_tensor(own_n, ident[:, 0:E], nvis, ALU.mult)
            link(v_.tensor_tensor_scan(hs[:, tail], ones[:, tail], heavy[:, tail], 0.0, ALU.mult, ALU.add))
            n_col = small[:, 432:436]
            v_.tensor_reduce(n_col[:, 0:1], own_n, AX.X, ALU.add)
            v_.tensor_copy(n_col[:, 2:3], hs[:, E - 1:E])
            v_.tensor_scalar(n_col[:, 3:4], hs[:, E - 1:E], -1.0, float(E - 1), ALU.mult, ALU.add)
            link(v_.tensor_tensor(h_at[:, tail], hs[:, tail], heavy[:, tail], ALU.subtract))
            link(v_.scalar_tensor_tensor(l_at[:, tail], iota[:, tail], 1.0, h_at[:, tail], ALU.subtract, ALU.subtract))
            v_.tensor_scalar(p_heavy[:, tail], h_at[:, tail], 1.0, n_col[:, 3:4], ALU.add, ALU.min)
            link(v_.tensor_scalar(p_light[:, tail], l_at[:, tail], n_col[:, 2:3], 1.0, ALU.min, ALU.add))
            v_.tensor_tensor(p_light[:, tail], p_light[:, tail], l_at[:, tail], ALU.add)
            link(v_.scalar_tensor_tensor(p_heavy[:, tail], h_at[:, tail], 1.0, p_heavy[:, tail], ALU.add, ALU.add))
            link(v_.tensor_tensor(p_heavy[:, tail], p_heavy[:, tail], p_light[:, tail], ALU.subtract))
            link(v_.tensor_tensor(p_heavy[:, tail], p_heavy[:, tail], heavy[:, tail], ALU.mult))
            v_.memset(order[:, 0:1], 0.0)
            link(v_.tensor_tensor(order[:, tail], p_light[:, tail], p_heavy[:, tail], ALU.add))
            link(v_.tensor_tensor(own_col, ident[:, 0:E], order, ALU.mult))
            link(v_.tensor_reduce(n_col[:, 1:2], own_col, AX.X, ALU.add))
            v_.tensor_scalar(first_rhs, order[0:E, :], n_col[0:E, 1:2], n_col[0:E, 0:1], ALU.is_gt, ALU.mult).then_inc(S["first_ready"], 1)
            dve.wait_ge(S["first_mm"], 1)
            link(v_.tensor_copy(vstart, bank[:, 5, E:2 * E]))
            v_.tensor_tensor(vend, vstart, nvis, ALU.add)
            dve.wait_ge(S["pos_mm"], 2)
            dve.wait_ge(S["sel_ready"], TOPK)
            link(v_.scalar_tensor_tensor(rw("code"), vstart.rearrange("p (a e) -> p a e", a=1).to_broadcast(shape), float(P),
                                         bank[:, 7, 0:P].rearrange("p (i e) -> p i e", i=TT), ALU.mult, ALU.add))
            code_k = small[:, 304:320]
            select("code", code_k)
            code_i, lo_i, hi_i = (small[:, 320 + 16 * n:336 + 16 * n].bitcast(I32) for n in range(3))
            link(v_.tensor_copy(code_i, code_k))
            v_.tensor_scalar(hi_i, code_i, 7, None, ALU.arith_shift_right)
            link(v_.tensor_scalar(lo_i, code_i, P - 1, None, ALU.bitwise_and))
            v_.tensor_copy(vis_k, hi_i)
            link(v_.tensor_copy(lo_k, lo_i))
            dve.wait_ge(S["lg_mm"], TT)
            for i in range(TT):
                qs = slice(TOPK * i, TOPK * (i + 1))

                def same(dst, of, n):
                    return v_.tensor_tensor(dst, iota[:, 0:n].rearrange("p (a n) -> p a n", a=1).to_broadcast([P, TOPK, n]),
                                            of[:, qs].rearrange("p (k a) -> p k a", a=1).to_broadcast([P, TOPK, n]), ALU.is_equal)

                same(hot_v[:, qs, NCOL:2 * NCOL], vis_k, NCOL).then_inc(S["dve_step"], 1)
                step[0] += 1
                same(hot_l[:, qs, :], lo_k, P)
                dve.wait_ge(S["dve_step"], step[0])
                link(v_.tensor_scalar(hot_v[:, qs, 0:NCOL], hot_v[:, qs, NCOL:2 * NCOL], tid[:, 0:1], None, ALU.mult))
                v_.tensor_scalar(hot_v[:, qs, NCOL:2 * NCOL], hot_v[:, qs, NCOL:2 * NCOL], float(i), None, ALU.mult).then_inc(S["hot_ready"], 1)
            dve.wait_ge(S["tab_mm"], 1)
            tile_part = small[:, 624:624 + NCOL]
            link(v_.tensor_scalar(tile_part, bank[:, 4, NCOL:2 * NCOL], float(P), None, ALU.mult))
            v_.tensor_tensor(tok[:, :], tile_part, bank[:, 4, 0:NCOL], ALU.add).then_inc(S["tok_ready"], 1)

            p_col = tid[:, 0:1]
            p128, expert, rest, owned, half_col, tid2 = (small[:, 368 + 4 * n:372 + 4 * n] for n in range(6))
            visit_cols = small[:, 392:396]
            last_end = small[:, 436:437]
            link(v_.tensor_reduce(last_end, vend, AX.X, ALU.max))
            link(v_.tensor_scalar(p128[:, 0:1], p_col, float(P), None, ALU.mult))
            link(v_.tensor_scalar(ended, vend, p_col, None, ALU.is_le))
            link(v_.scalar_tensor_tensor(own, vstart, p_col, ended, ALU.is_le, ALU.subtract))
            v_.tensor_scalar(here, order, p_col, None, ALU.is_equal)
            v_.tensor_scalar(owned[:, 0:1], p_col, last_end, None, ALU.is_lt)
            link(v_.scalar_tensor_tensor(part, vstart, float(P), cnt, ALU.mult, ALU.add))
            v_.tensor_tensor(own_col, own, order, ALU.mult)
            v_.tensor_tensor(own_n, here, iota[:, 0:E], ALU.mult)
            v_.scalar_tensor_tensor(p_heavy, vend, 1.0, here, ALU.subtract, ALU.mult)
            link(v_.scalar_tensor_tensor(part, part, p128[:, 0:1], own, ALU.subtract, ALU.mult))
            v_.tensor_reduce(expert[:, 0:1], own_col, AX.X, ALU.add)
            v_.tensor_reduce(visit_cols[:, 2:3], own_n, AX.X, ALU.add)
            v_.tensor_reduce(visit_cols[:, 3:4], p_heavy, AX.X, ALU.add)
            link(v_.tensor_reduce(rest[:, 0:1], part, AX.X, ALU.add))
            v_.tensor_scalar(visit_cols[:, 1:2], expert[:, 0:1], 16.0, 16.0, ALU.mult, ALU.add)
            v_.scalar_tensor_tensor(visit_cols[:, 0:1], rest[:, 0:1], float(BLK), owned[:, 0:1], ALU.is_gt, ALU.add).then_inc(S["visit_cols"], 1)
            dve.wait_ge(S["visit_mm"], 1)
            v_.tensor_copy(visits[:, :, :], bank[0:1, 6, P:P + 4 * NCOL].rearrange("p (a n) -> p a n", a=4)).then_inc(S["visits_ready"], 1)

            dve.wait_ge(S["r_exp"], 1)
            link(v_.tensor_tensor(rw("ex"), rw("ex"), rw("mask"), ALU.mult))
            link(v_.tensor_reduce(small[:, 36:40], rw("ex"), AX.X, ALU.add))
            link(v_.reciprocal(small[:, 40:44], small[:, 36:40]))
            link(v_.tensor_tensor(rw("gate"), rw("ex"), small[:, 40:44].rearrange("p (i a) -> p i a", a=1).to_broadcast(shape), ALU.mult))
            gate_k = small[:, 288:304]
            select("gate", gate_k)
            link(v_.tensor_scalar(hi_i, code_i, 6, None, ALU.arith_shift_right))
            link(v_.tensor_scalar(lo_i, code_i, BLK - 1, None, ALU.bitwise_and))
            block_k, in_k = small[:, 400:416], small[:, 416:432]
            v_.tensor_copy(block_k, hi_i)
            v_.tensor_copy(in_k, lo_i)
            link(v_.tensor_scalar(half_col[:, 0:1], p_col, float(BLK), None, ALU.is_ge))
            link(v_.tensor_tensor(half_col[:, 1:2], half_col[:, 0:1], p_col, ALU.subtract))
            link(v_.tensor_scalar(tid2, tid[:, :], 2.0, float(P), ALU.mult, ALU.add))
            for q in range(TT * TOPK):
                v_.tensor_scalar(hot2_l[:, q, :, :], iota[:, 0:BLK].rearrange("p (a n) -> p a n", a=1).to_broadcast([P, 2, BLK]),
                                 in_k[:, q:q + 1], None, ALU.is_equal)
                v_.tensor_scalar(hot2_v[:, q, 0:2 * NCOL], iota[:, 0:2 * NCOL], block_k[:, q:q + 1], tid2[:, q // TOPK:q // TOPK + 1],
                                 ALU.is_equal, ALU.mult)
                v_.tensor_scalar(hot2_v[:, q, 2 * NCOL:4 * NCOL], iota[:, 0:2 * NCOL], block_k[:, q:q + 1], gate_k[:, q:q + 1],
                                 ALU.is_equal, ALU.mult).then_inc(S["hot2_ready"], 1)

            def swiglu(v, nb, first=False):
                dve.wait_ge(S["win_used"], 8 * (v + 1))
                v_.tensor_scalar(g_sb[:, 0:nb, :], bank[:, 0:nb, :], LIMIT, None, ALU.min).then_inc(S["g_ready"], 1)
                v_.tensor_scalar(l_sb[:, 0:nb, :], bank[:, 2:2 + nb, :], LIMIT, -LIMIT, ALU.min, ALU.max).then_inc(S["u_free"], 1)
                dve.wait_ge(S["g_ready"], v + 1)
                dve.wait_ge(S["u_free"], v + 1)
                v_.scalar_tensor_tensor(l_sb[:, 0:nb, :], l_sb[:, 0:nb, :], 1.0, g_sb[:, 0:nb, :], ALU.add, ALU.mult).then_inc(S["lin_done"], 1)
                dve.wait_ge(S["lin_done"], v + 1)
                dve.wait_ge(S["s_ready"], v + 1)
                if not first:
                    dve.wait_ge(S["atr_done"], v)
                v_.tensor_tensor(act_a[:, 0:nb, :], l_sb[:, 0:nb, :], s_sb[:, 0:nb, :], ALU.mult).then_inc(S["a_ready"], 1)

            def by_blocks(v, f):
                n = dve.value_load(visits[0:1, 0, bass.ds(v, 1)], min_val=0, max_val=2)
                with dve.If(n > 1):
                    f(2)
                with dve.Else():
                    f(1)

            by_blocks(0, lambda nb: swiglu(0, nb, True))
            dve.wait_ge(S["tab2_mm"], 1)
            shift = mrow[:, 0, 0:2 * NCOL]
            link(v_.tensor_scalar(shift, bank[:, 7, 0:2 * NCOL], 0.0, half_col[:, 1:2], ALU.is_gt, ALU.mult))
            link(v_.scalar_tensor_tensor(row_col[:, :], bank[:, 7, 0:2 * NCOL], tid[:, 0:1], shift, ALU.add, ALU.add))
            v_.tensor_copy(gate_col[:, :], bank[:, 7, 2 * NCOL:4 * NCOL]).then_inc(S["col_ready"], 1)
            with dve.Fori(1, E) as v:
                by_blocks(v, lambda nb: swiglu(v, nb))
            with dve.Fori(0, GROUPS) as group:
                some = dve.value_load(visits[0:1, 0, bass.ds(group * (2 * PAIRS) + E, 1)], min_val=0, max_val=2)
                with dve.If(some > 0):
                    with dve.Fori(0, 2 * PAIRS) as member:
                        v = group * (2 * PAIRS) + member + E
                        n = dve.value_load(visits[0:1, 0, bass.ds(v, 1)], min_val=0, max_val=2)
                        with dve.If(n > 0):
                            by_blocks(v, lambda nb: swiglu(v, nb))

            dve.wait_ge(S["bc_in"], 16 * 4)
            def residual(i):
                dve.wait_ge(S["fin_rstd"], i + 1)
                v_.scalar_tensor_tensor(x1[:, i, :], fin_t(i), stat[:, 56 + i:57 + i], x1[:, i, :], ALU.mult, ALU.add).then_inc(S["fin_done"], 1)

            for i in range(TT):
                dve.wait_ge(fin_in[i], 32)
                v_.tensor_tensor(fin_y(i), fin_y(i), fin_z(i), ALU.add).then_inc(S["yacc"], 1)
                dve.wait_ge(S["yacc"], i + 1)
                link(v_.tensor_tensor(fin_t(i), fin_y(i), gm[:, :], ALU.mult))
                if i >= 1:
                    residual(i - 1)
            residual(TT - 1)

        @block.tensor
        def _(pe):
            t_ = nc.tensor

            def turn(dst, src, n=P):
                return t_.transpose(dst, src, ident[0:n, 0:n])

            pe.wait_ge(S["small_in"], 16 * 6)
            pe.wait_ge(S["consts"], 1)
            turn(bank[:, 3, 0:82], vrows[:, :], 82).then_inc(S["vr_done"], 1)
            pe.wait_ge(S["csT_done"], 1)
            turn(bank[:, 2, 0:KT], crow[:, :], KT).then_inc(S["vr_done"], 1)
            pe.wait_ge(S["csT_ev"], 1)

            def ada_rows(n):
                s = at_chunk[("ada", n)]
                pe.wait_ge(stream[s % 3], 16 * (s // 3 + 1))
                if n >= 2:
                    pe.wait_ge(S["ada_row"], n - 1)
                w = chunk_buf(s)
                for k in range(KT):
                    for q in range(4):
                        ins = t_.matmul(bank[32 * q:32 * q + 32, ada_bank(n), 0:P], lhsT=cs_pad[:, k, :], rhs=w[:, k, q * P:(q + 1) * P],
                                        start=(k == 0), stop=(k == KT - 1), tile_position=(0, 32 * q))
                ins.then_inc(S["ada_mm"], 1)

            def ada_turn(n):
                pe.wait_ge(S["ada_row"], n + 1)
                if n >= 2:
                    pe.wait_ge(S["ada_col"], n - 1)
                turn(bank[:, ada_bank(n) + 2, 0:P], mrow[:, n % 2, :]).then_inc(S["ada_tr"], 1)

            def turn_xn(k):
                if k >= 4:
                    pe.wait_ge(S["ht_act"] if k % 2 else S["ht_dve"], (k - 4) // 2 + 1)
                for i in range(TT):
                    ins = turn(bank[:, 4 + k % 4, i * P:(i + 1) * P], x_sb[:, i, k * P:(k + 1) * P])
                ins.then_inc(S["xt_mm"], 1)

            for n in range(3):
                ada_rows(n)
                ada_turn(n)
            pe.wait_ge(S["x_norm"], TT)
            for k in range(4):
                turn_xn(k)
            ada_rows(3)
            ada_turn(3)
            for k in range(4, KT):
                turn_xn(k)
            pe.wait_ge(S["ht_act"], 4)
            pe.wait_ge(S["ht_dve"], 4)
            pe.wait_ge(S["ada_col"], 4)
            pe.wait_ge(S["fx_in"], 16 * 7)

            for j, (kind, a, who) in enumerate(outs):
                if j >= 4:
                    pe.wait_ge(*taken(j - 4))
                base = {"qg": C_QG, "kg": C_QG, "gg": C_GG, "vg": C_VG, "kf": C_KF, "qf": C_QF, "vf": C_VF}.get(kind)
                if base is not None:
                    s = at_chunk[("in", base)]
                    pe.wait_ge(stream[s % 3], 16 * (s // 3 + 1))
                    w = chunk_buf(s)
                if kind == "gk":
                    pe.wait_ge(*taken(out_at[("zf", 0)]))
                    ins = t_.matmul(bank[:, j % 4, :], lhsT=wgk[:, a * P:(a + 1) * P], rhs=zf[0:LR, :], start=True, stop=True)
                for k in range(KT if kind != "gk" else 0):
                    if kind == "zf":
                        dst, lhsT, rhs = bank[0:40, j % 4, :], wzf[:, k, :], hT[:, k, :]
                    elif kind in ("qg", "kg", "kf", "qf"):
                        at = a * P + (256 if kind == "kg" else 0)
                        dst, lhsT, rhs = bank[:, j % 4, :], w[:, k, at:at + P], hT[:, k, :]
                    else:
                        dst, lhsT, rhs = bank[:, j % 4, :], hT[:, k, a * P:(a + 1) * P], w[:, k, :]
                    ins = t_.matmul(dst, lhsT=lhsT, rhs=rhs, start=(k == 0), stop=(k == KT - 1))
                ins.then_inc(S["proj_mm"], 1)
                for n in range(4, 12):
                    if ada_behind[n] == j:
                        ada_rows(n)
                for n in range(4, 12):
                    if ada_turned[n] == j:
                        ada_turn(n)
            for back in range(4):
                pe.wait_ge(*taken(len(outs) - 1 - back))

            pe.wait_ge(S["gla_ready"], 2)
            pe.wait_ge(S["ada_col"], 12)
            wait_out(pe, "vg")

            def gla_scores(i):
                cols_ = slice(i * P, (i + 1) * P)
                if i >= 1:
                    pe.wait_ge(S["kd_ev"], i)
                for a in range(2):
                    ins = turn(bank[:, 2, a * P:(a + 1) * P], kdT[:, a, cols_])
                ins.then_inc(S["kd_mm"], 1)
                if i >= 2:
                    pe.wait_ge(S["att_cp"], i - 1)
                for h in range(GH):
                    ins = t_.matmul(bank[:, i % 2, h * P:(h + 1) * P], lhsT=ktT[:, h // 2, cols_], rhs=qtp[:, h, cols_],
                                    start=True, stop=True)
                ins.then_inc(S["att_mm"], 1)

            def gla_out(i):
                pe.wait_ge(S["kd_ev"], i + 1)
                if i == 0:
                    pe.wait_ge(S["consts"], 3)
                else:
                    pe.wait_ge(S["st_done"], 2 * i)
                for ch in range(2 if i < TT - 1 else 1):
                    for a in range(2):
                        ins = t_.matmul(bank[:, 3 + ch, a * 256:(a + 1) * 256], lhsT=kdz[:, i % 2, ch, a * P:(a + 1) * P],
                                        rhs=vg[:, i, a * 256:(a + 1) * 256], start=True, stop=True)
                    ins.then_inc(S["kv_mm"], 1)
                pe.wait_ge(S["att_ready"], i + 1)
                if i >= 2:
                    pe.wait_ge(S["go_ev"], i - 1)
                pe.wait_ge(S["st_done"], 2 * i + 1)
                ob = bank[:, 5 + i % 2, :]
                for h in range(GH):
                    hs = slice(h * P, (h + 1) * P)
                    t_.matmul(ob[:, hs], lhsT=attz[:, i % 2, h, :], rhs=vg[:, i, hs], start=True, stop=False, skip_group_check=True)
                    for ch in range(2):
                        r = slice(64 * ch, 64 * ch + 64)
                        ins = t_.matmul(ob[r, hs], lhsT=qtp[:, h, i * P + 64 * ch:i * P + 64 * ch + 64],
                                        rhs=state[:, (2 * i + ch) % 4, h, :], start=False, stop=True, skip_group_check=True)
                ins.then_inc(S["go_mm"], 1)

            gla_scores(0)
            pe.wait_ge(S["cols_ready"], 1)
            turn(bank[0:32, 7, 0:P], cols[:, :, :].rearrange("p a k -> p (a k)")).then_inc(S["colT_mm"], 1)
            for i in range(TT):
                if i + 1 < TT:
                    gla_scores(i + 1)
                gla_out(i)

            pe.wait_ge(S["fx_in"], 16 * 9)
            wait_out(pe, "kf")
            wait_out(pe, "qf")
            wait_out(pe, "vf")
            pe.wait_ge(S["consts"], 2)

            def fox_scores(u):
                qi, h = units[u]
                if u >= 3:
                    pe.wait_ge(S["exp_done"], u - 2)
                elif u == 0:
                    pe.wait_ge(S["att_cp"], TT)
                    pe.wait_ge(S["kd_ev"], TT)
                n = (qi + 1) * P
                t_.matmul(bank[:, u % 3, 0:n], lhsT=qa[:, h, qi * P:n], rhs=ka[:, h, 0:n], start=True, stop=False, skip_group_check=True)
                t_.matmul(bank[:, u % 3, qi * P:n], lhsT=identb[:, :], rhs=maskb[:, :], start=False, stop=True,
                          skip_group_check=True).then_inc(S["s_done"], 1)

            def fox_turn(u):
                qi, h = units[u]
                pe.wait_ge(S["norm_done"], u + 1)
                if u >= 2:
                    pe.wait_ge(S["pt_ev"], u - 1)
                else:
                    pe.wait_ge(S["st_done"], 7)
                for kb in range(qi + 1):
                    ins = turn(bank[:, 3 + u % 2, kb * P:(kb + 1) * P], probs[u % 3][:, kb * P:(kb + 1) * P])
                ins.then_inc(S["pt_done"], 1)

            def fox_values(u):
                qi, h = units[u]
                pe.wait_ge(S["pt_ev"], u + 1)
                if h == 0:
                    if qi >= 2:
                        pe.wait_ge(S["mixf"], qi - 1)
                    else:
                        pe.wait_ge(S["go_ev"], 3 + qi)
                for kb in range(qi + 1):
                    ins = t_.matmul(bank[64 * (h % 2):64 * (h % 2) + 64, 5 + qi % 2, (h // 2) * P:(h // 2 + 1) * P],
                                    lhsT=vf[:, kb, h * FD:(h + 1) * FD], rhs=probT[:, u % 2, kb * P:(kb + 1) * P],
                                    start=(kb == 0), stop=(kb == qi), tile_position=(0, 64 * (h % 2)), skip_group_check=True)
                ins.then_inc(S["pv_done"], 1)

            def mix_turn(qi):
                pe.wait_ge(S["mixg"], qi + 1)
                if qi:
                    pe.wait_ge(S["mt_ev"], qi)
                else:
                    pe.wait_ge(S["vec_ready"], 1)
                for k in range(4):
                    ins = turn(bank[:, 7, k * P:(k + 1) * P], mix[:, qi, k * P:(k + 1) * P])
                ins.then_inc(S["mt_mm"], 1)

            for w in range(len(units) + 3):
                if w < len(units):
                    fox_scores(w)
                if 2 <= w <= len(units) + 1:
                    fox_turn(w - 2)
                if w >= 3:
                    fox_values(w - 3)
                if w % 8 == 5 and w < len(units):
                    mix_turn(w // 8)

            pe.wait_ge(S["wo_in"], 16)

            def project(i):
                pe.wait_ge(S["mt_ev"], TT)
                pe.wait_ge(S["mixf"], TT)
                if i >= 2:
                    pe.wait_ge(S["x1_done"], i - 1)
                elif i == 0:
                    pe.wait_ge(S["exp_done"], len(units))
                    pe.wait_ge(S["pt_ev"], len(units))
                for n in range(2):
                    for k in range(KT):
                        ins = t_.matmul(bank[:, 2 * (i % 2) + n, :], lhsT=mixT[:, k, i * P:(i + 1) * P],
                                        rhs=wo_sb[:, k, n * 512:(n + 1) * 512], start=(k == 0), stop=(k == KT - 1))
                ins.then_inc(S["wo_mm"], 1)

            def logits(i):
                pe.wait_ge(S["h2_done"], i + 1)
                if i >= 1:
                    pe.wait_ge(S["h2t_ev"], i)
                for k in range(KT):
                    ins = turn(bank[:, 4 + k // 4, (k % 4) * P:(k % 4 + 1) * P], h2[:, i % 2, k * P:(k + 1) * P])
                ins.then_inc(S["h2t_mm"], 1)
                pe.wait_ge(S["h2t_ev"], i + 1)
                if i >= 1:
                    pe.wait_ge(S["lg_done"], i)
                for k in range(KT):
                    ins = t_.matmul(bank[:, 6, i * E:(i + 1) * E], lhsT=h2T[:, i % 2, k, :], rhs=w_r[:, k, :],
                                    start=(k == 0), stop=(k == KT - 1))
                ins.then_inc(S["lg_mm"], 1)

            for i in range(TT):
                project(i)
                if i >= 1:
                    logits(i - 1)
            logits(TT - 1)

            pe.wait_ge(S["r_mask"], 1)
            for j in range(TT):
                ins = t_.matmul(bank[:, 5, 0:E], lhsT=ones[:, :], rhs=mask_bf[:, j * E:(j + 1) * E], start=(j == 0), stop=(j == TT - 1))
            ins.then_inc(S["pos_mm"], 1)
            for i in range(TT):
                for j in range(i + 1):
                    ins = t_.matmul(bank[:, 7, i * E:(i + 1) * E], lhsT=before[:, :] if j == i else ones[:, :],
                                    rhs=mask_bf[:, j * E:(j + 1) * E], start=(j == 0), stop=(j == i))
            ins.then_inc(S["pos_mm"], 1)
            pe.wait_ge(S["first_ready"], 1)
            t_.matmul(bank[:, 5, E:2 * E], lhsT=ones[0:E, :], rhs=first_rhs, start=True, stop=True).then_inc(S["first_mm"], 1)
            for q in range(TT * TOPK):
                pe.wait_ge(S["hot_ready"], q // TOPK + 1)
                ins = t_.matmul(bank[:, 4, 0:2 * NCOL], lhsT=hot_l[:, q, :], rhs=hot_v[:, q, :], start=(q == 0), stop=(q == TT * TOPK - 1))
            ins.then_inc(S["tab_mm"], 1)
            pe.wait_ge(S["visit_cols"], 1)
            for n in range(4):
                ins = t_.matmul(bank[0:1, 6, P + NCOL * n:P + NCOL * (n + 1)], lhsT=small[:, 392 + n:393 + n], rhs=ident[:, 0:NCOL],
                                start=True, stop=True)
            ins.then_inc(S["visit_mm"], 1)

            def turn_x(v, parity, nb, first=False):
                pe.wait_ge(gathered[parity], (v - parity) * 8 + 16)
                if not first:
                    pe.wait_ge(S["at_ready"], v - 1)
                n = BLK * nb
                if nb == 1:
                    t_.matmul(bank[0:1, 4, 0:1], lhsT=ident[:, 0:1], rhs=ident[:, 0:1], start=True, stop=True)
                for k in range(KT):
                    ins = turn(bank[:, 4 + k // 4, (k % 4) * P:(k % 4) * P + n], xg[parity][0:n, k * P:(k + 1) * P], n)
                    if k % 4 == 3:
                        ins.then_inc(S["xtr_done"], 1)

            def weights_in(v):
                return pe.value_load(visits[0:1, 1, bass.ds(v, 1)], min_val=16, max_val=16 * (E + 1))

            def up(v, nb, first=False):
                pe.wait_ge(S["xt_ready"], 2 * v + 2)
                w_in_at = weights_in(v)
                pe.wait_ge(S["up_bias_in"], w_in_at)
                if not first:
                    pe.wait_ge(S["u_free"], v)
                for b in range(nb):
                    for g in range(2):
                        for half in range(2):
                            ins = t_.matmul(bank[64 * half:64 * half + 64, 2 * g + b, :], lhsT=ones3[:, :],
                                            rhs=bup[:, g * D + half * 512:g * D + half * 512 + 512], start=True, stop=False,
                                            tile_position=(0, 64 * half), skip_group_check=True)
                ins.then_inc(S["up_bias_used"], 1)
                for k in range(KT):
                    pe.wait_ge(w_slot[k], w_in_at)
                    for b in range(nb):
                        for g in range(2):
                            for half in range(2):
                                ins = t_.matmul(bank[64 * half:64 * half + 64, 2 * g + b, :],
                                                lhsT=xT[:, k, BLK * b:BLK * b + BLK],
                                                rhs=slot(k)[:, g * D + half * 512:g * D + half * 512 + 512],
                                                start=False, stop=(k == KT - 1), tile_position=(0, 64 * half), skip_group_check=True)
                    ins.then_inc(S["win_used"], 1)

            def turn_a(v, nb):
                pe.wait_ge(S["a_ready"], v + 1)
                pe.wait_ge(S["xt_ready"], 2 * v + 4)
                for b in range(nb):
                    for q in range(4):
                        ins = turn(bank[:, 4 + b, q * P:(q + 1) * P], act_a[:, b, q * P:(q + 1) * P])
                ins.then_inc(S["atr_done"], 1)

            def down(v, nb, first=False):
                pe.wait_ge(S["at_ready"], v + 1)
                w_in_at = weights_in(v)
                pe.wait_ge(S["dn_bias_in"], w_in_at)
                if not first:
                    pe.wait_ge(S["y_evac"], v)
                for b in range(nb):
                    for half in range(2):
                        ins = t_.matmul(bank[64 * half:64 * half + 64, 6 + b, :], lhsT=ones3[:, :],
                                        rhs=bdn[:, half * 512:half * 512 + 512], start=True, stop=False,
                                        tile_position=(0, 64 * half), skip_group_check=True)
                ins.then_inc(S["dn_bias_used"], 1)
                for j in range(4):
                    pe.wait_ge(w_slot[8 + j], w_in_at)
                    for kk in range(2):
                        kt = 2 * j + kk
                        for b in range(nb):
                            for half in range(2):
                                ins = t_.matmul(bank[64 * half:64 * half + 64, 6 + b, :],
                                                lhsT=aT[:, b, kt % 4, BLK * (kt // 4):BLK * (kt // 4) + BLK],
                                                rhs=slot(8 + j)[:, kk * D + half * 512:kk * D + half * 512 + 512],
                                                start=False, stop=(kt == KT - 1), tile_position=(0, 64 * half), skip_group_check=True)
                    ins.then_inc(S["wout_used"], 1)

            def by_blocks(v, f):
                n = pe.value_load(visits[0:1, 0, bass.ds(v, 1)], min_val=0, max_val=2)
                with pe.If(n > 1):
                    f(2)
                with pe.Else():
                    f(1)

            turn_x(0, 0, 2, True)
            pe.wait_ge(S["visits_ready"], 1)
            by_blocks(0, lambda nb: up(0, nb, True))
            pe.wait_ge(S["hot2_ready"], TT * TOPK)
            for q in range(TT * TOPK):
                ins = t_.matmul(bank[:, 7, 0:4 * NCOL], lhsT=hot2_l[:, q, :, :], rhs=hot2_v[:, q, :], start=(q == 0), stop=(q == TT * TOPK - 1))
            ins.then_inc(S["tab2_mm"], 1)
            pe.wait_ge(S["xt_ready"], 2)
            by_blocks(1, lambda nb: turn_x(1, 1, nb, True))
            pe.wait_ge(S["xt_ready"], 4)
            by_blocks(0, lambda nb: turn_a(0, nb))
            by_blocks(1, lambda nb: up(1, nb))
            by_blocks(2, lambda nb: turn_x(2, 0, nb))
            pe.wait_ge(S["col_ready"], 1)
            by_blocks(0, lambda nb: down(0, nb, True))
            with pe.Fori(1, E // 2) as pair:
                for parity in range(2):
                    v = pair * 2 + parity
                    by_blocks(v - 1, lambda nb: turn_a(v - 1, nb))
                    by_blocks(v, lambda nb: up(v, nb))
                    by_blocks(v + 1, lambda nb: turn_x(v + 1, 1 - parity, nb))
                    by_blocks(v - 1, lambda nb: down(v - 1, nb))
            by_blocks(E - 1, lambda nb: (turn_a(E - 1, nb), down(E - 1, nb)))

            def extra(v, parity, then=None):
                n = pe.value_load(visits[0:1, 0, bass.ds(v, 1)], min_val=0, max_val=2)
                with pe.If(n > 0):
                    by_blocks(v, lambda nb: up(v, nb))
                    by_blocks(v + 1, lambda nb: turn_x(v + 1, 1 - parity, nb))
                    by_blocks(v, lambda nb: (turn_a(v, nb), down(v, nb)))
                    if then:
                        then()

            with pe.Fori(0, GROUPS) as group:
                some = pe.value_load(visits[0:1, 0, bass.ds(group * (2 * PAIRS) + E, 1)], min_val=0, max_val=2)
                with pe.If(some > 0):
                    with pe.Fori(0, PAIRS) as pair:
                        v = group * (2 * PAIRS) + pair * 2 + E
                        extra(v, 0, lambda: extra(v + 1, 1))


_INS = ['x', 'c', 'w_ada', 'b_ada', 'attn_pre_gain', 'attn_post_gain', 'w_in', 'w_gk2', 'b_gk', 'gla_norm_gain',
        'b_f', 'w_o', 'mlp_pre_gain', 'mlp_post_gain', 'w_router', 'b_router', 'w_e_in', 'b_e_in', 'w_e_out', 'b_e_out']


def kernel(**inputs):
    import numpy as _np
    import concourse.bacc as _bacc
    from concourse import mybir as _mybir
    from concourse.bass_utils import run_bass_kernel_spmd as _run

    nc = _bacc.Bacc("TRN2", target_bir_lowering=False, num_devices=1)
    arrays, args = {}, []
    for name in _INS:
        a = _np.ascontiguousarray(inputs[name])
        arrays[f"in_{name}_dram"] = a
        args.append(nc.dram_tensor(f"in_{name}_dram", a.shape, _mybir.dt.from_np(a.dtype), kind="ExternalInput").ap())
    out = nc.dram_tensor("out_0_dram", (1, T, D), _mybir.dt.float32, kind="ExternalOutput").ap()
    build(nc, *args, out)
    r = _run(nc, [arrays], core_ids=[0])
    return r.results[0]["out_0_dram"]
```
